# Optimizing a Trainium2 kernel written in Bass

```python
import math
import jax, jax.numpy as jnp
from jax import lax
import numpy as np

D_MODEL = 1024
BATCH = 1
SEQ = 512
DEPTH = 1

D_RNN = D_MODEL // 2
N_RNN_BLOCKS = 8
RNN_BLOCK = D_RNN // N_RNN_BLOCKS
CONV_WIDTH = 4
LRU_C = 8.0
DIFF_HEAD_DIM = 64
N_DIFF_HEADS = (D_MODEL // 2) // (2 * DIFF_HEAD_DIM)
D_ATTN = N_DIFF_HEADS * 2 * DIFF_HEAD_DIM
D_MIX = D_RNN + D_ATTN
D_IN = 2 * D_RNN + 3 * D_ATTN
Q_BLOCK = 128
N_EXPERTS = 32
TOP_K = 4
D_FF = D_MODEL
SWIGLU_LIMIT = 7.0
SWIGLU_ALPHA = 1.702
MOE_BLOCK = 128
EPS = 1e-5

kernel_name = "hybrid_rglru_diffattn_moe"

def rms_norm(x, g):
    xf = x.astype(jnp.float32)
    y = xf * lax.rsqrt(jnp.mean(xf * xf, axis=-1, keepdims=True) + EPS)
    return (y * g.astype(jnp.float32)).astype(x.dtype)

def causal_depthwise_conv(x, w, b):
    c = x.shape[-1]
    y = lax.conv_general_dilated(
        x, w[:, None, :].astype(x.dtype), window_strides=(1,),
        padding=[(CONV_WIDTH - 1, 0)], dimension_numbers=("NWC", "WIO", "NWC"),
        feature_group_count=c)
    return y + b

def _lru_combine(left, right):
    a_l, h_l = left
    a_r, h_r = right
    return a_l * a_r, a_r * h_l + h_r

def rg_lru(x, w_a, b_a, w_x, b_x, lam):
    bsz, seq, _ = x.shape
    xb = x.reshape(bsz, seq, N_RNN_BLOCKS, RNN_BLOCK)
    r = jax.nn.sigmoid(jnp.einsum("bsni,nij->bsnj", xb, w_a).reshape(bsz, seq, D_RNN) + b_a)
    i = jax.nn.sigmoid(jnp.einsum("bsni,nij->bsnj", xb, w_x).reshape(bsz, seq, D_RNN) + b_x)
    log_a = -LRU_C * r.astype(jnp.float32) * jax.nn.softplus(-lam.astype(jnp.float32))
    a = jnp.exp(log_a)
    u = jnp.sqrt(-jnp.expm1(2.0 * log_a)) * (i * x).astype(jnp.float32)
    _, h = lax.associative_scan(_lru_combine, (a, u), axis=1)
    return h.astype(x.dtype)

def diff_attention(q, k, v, lam):
    bsz, seq = q.shape[:2]
    nb = seq // Q_BLOCK
    q = jnp.transpose(q, (0, 2, 3, 1, 4))
    k = jnp.transpose(k, (0, 2, 3, 1, 4))
    v = jnp.transpose(v, (0, 2, 1, 3))
    qb = jnp.moveaxis(q.reshape(bsz, N_DIFF_HEADS, 2, nb, Q_BLOCK, DIFF_HEAD_DIM), 3, 0)
    kpos = jnp.arange(seq)

    def one_block(args):
        q_blk, blk = args
        s = jnp.einsum("bhcqd,bhckd->bhcqk", q_blk, k).astype(jnp.float32)
        qpos = blk * Q_BLOCK + jnp.arange(Q_BLOCK)
        s = jnp.where(kpos[None, :] <= qpos[:, None], s, -jnp.inf)
        p = jax.nn.softmax(s, axis=-1)
        w = p[:, :, 0] - lam * p[:, :, 1]
        return jnp.einsum("bhqk,bhke->bhqe", w.astype(v.dtype), v)

    o = lax.map(one_block, (qb, jnp.arange(nb)))
    return jnp.transpose(o, (1, 0, 3, 2, 4)).reshape(bsz, seq, N_DIFF_HEADS, 2 * DIFF_HEAD_DIM)

def moe_ffn(h, router_w, router_b, w1, b1, w2, b2):
    bsz, seq, d = h.shape
    n_tok = bsz * seq
    xt = h.reshape(n_tok, d)
    logits = jnp.dot(xt.astype(jnp.float32), router_w.astype(jnp.float32)) + router_b.astype(jnp.float32)
    top_val, top_idx = lax.top_k(logits, TOP_K)
    gates = jax.nn.softmax(top_val, axis=-1).reshape(-1)
    flat_e = top_idx.reshape(-1)
    n_asg = n_tok * TOP_K
    order = jnp.argsort(flat_e)
    sorted_e = flat_e[order]
    tok = order // TOP_K
    counts = jnp.bincount(flat_e, length=N_EXPERTS)
    padded = (counts + MOE_BLOCK - 1) // MOE_BLOCK * MOE_BLOCK
    pad_end = jnp.cumsum(padded)
    pad_start = pad_end - padded
    grp_start = jnp.cumsum(counts) - counts
    dest = pad_start[sorted_e] + jnp.arange(n_asg) - grp_start[sorted_e]
    n_blocks = (n_asg + MOE_BLOCK - 1) // MOE_BLOCK + N_EXPERTS
    src = jnp.full((n_blocks * MOE_BLOCK,), n_asg, dtype=jnp.int32).at[dest].set(
        jnp.arange(n_asg, dtype=jnp.int32))
    x_sorted = jnp.concatenate([xt[tok], jnp.zeros((1, d), xt.dtype)], axis=0)
    x_blocks = x_sorted[src].reshape(n_blocks, MOE_BLOCK, d)
    blk_e = jnp.minimum(jnp.searchsorted(pad_end, jnp.arange(n_blocks) * MOE_BLOCK, side="right"),
                        N_EXPERTS - 1)

    def expert_block(args):
        xb, e = args
        hcat = xb @ w1[e] + b1[e]
        gate = jnp.minimum(hcat[:, :D_FF], SWIGLU_LIMIT)
        up = jnp.clip(hcat[:, D_FF:], -SWIGLU_LIMIT, SWIGLU_LIMIT)
        act = gate * jax.nn.sigmoid(SWIGLU_ALPHA * gate) * (up + 1.0)
        return act @ w2[e] + b2[e]

    y_blocks = lax.map(expert_block, (x_blocks, blk_e)).reshape(-1, d)
    y_sorted = y_blocks[dest] * gates[order][:, None].astype(y_blocks.dtype)
    y = jax.ops.segment_sum(y_sorted, tok, num_segments=n_tok)
    return y.reshape(bsz, seq, d)

def setup_inputs(seed: int = 0) -> dict:
    key = jax.random.key(seed)
    ks = jax.random.split(key, 25)

    def nrm(k, shape, scale):
        return jax.random.normal(k, shape, jnp.float32) * scale

    a_c = jax.random.uniform(ks[9], (DEPTH, D_RNN), jnp.float32, minval=0.9, maxval=0.999)
    s = a_c ** (1.0 / LRU_C)
    return {
        "x": nrm(ks[0], (BATCH, SEQ, D_MODEL), 1.0),
        "norm1_g": 1.0 + nrm(ks[1], (DEPTH, D_MODEL), 0.02),
        "w_in": nrm(ks[2], (DEPTH, D_MODEL, D_IN), D_MODEL ** -0.5),
        "conv_w": nrm(ks[3], (DEPTH, CONV_WIDTH, D_RNN), CONV_WIDTH ** -0.5),
        "conv_b": nrm(ks[4], (DEPTH, D_RNN), 0.02),
        "lru_wa": nrm(ks[5], (DEPTH, N_RNN_BLOCKS, RNN_BLOCK, RNN_BLOCK), RNN_BLOCK ** -0.5),
        "lru_ba": nrm(ks[6], (DEPTH, D_RNN), 0.02),
        "lru_wx": nrm(ks[7], (DEPTH, N_RNN_BLOCKS, RNN_BLOCK, RNN_BLOCK), RNN_BLOCK ** -0.5),
        "lru_bx": nrm(ks[8], (DEPTH, D_RNN), 0.02),
        "lru_lambda": jnp.log(s) - jnp.log1p(-s),
        "q_norm_g": 1.0 + nrm(ks[10], (DEPTH, DIFF_HEAD_DIM), 0.02),
        "k_norm_g": 1.0 + nrm(ks[11], (DEPTH, DIFF_HEAD_DIM), 0.02),
        "lambda_q1": nrm(ks[12], (DEPTH, DIFF_HEAD_DIM), 0.1),
        "lambda_k1": nrm(ks[13], (DEPTH, DIFF_HEAD_DIM), 0.1),
        "lambda_q2": nrm(ks[14], (DEPTH, DIFF_HEAD_DIM), 0.1),
        "lambda_k2": nrm(ks[15], (DEPTH, DIFF_HEAD_DIM), 0.1),
        "subln_g": 1.0 + nrm(ks[16], (DEPTH, 2 * DIFF_HEAD_DIM), 0.02),
        "w_out": nrm(ks[17], (DEPTH, D_MIX, D_MODEL), D_MIX ** -0.5),
        "norm2_g": 1.0 + nrm(ks[18], (DEPTH, D_MODEL), 0.02),
        "router_w": nrm(ks[19], (DEPTH, D_MODEL, N_EXPERTS), D_MODEL ** -0.5),
        "router_b": nrm(ks[20], (DEPTH, N_EXPERTS), 0.01),
        "w1": nrm(ks[21], (DEPTH, N_EXPERTS, D_MODEL, 2 * D_FF), D_MODEL ** -0.5),
        "b1": nrm(ks[22], (DEPTH, N_EXPERTS, 2 * D_FF), 0.02),
        "w2": nrm(ks[23], (DEPTH, N_EXPERTS, D_FF, D_MODEL), D_FF ** -0.5),
        "b2": nrm(ks[24], (DEPTH, N_EXPERTS, D_MODEL), 0.02),
    }

def reference(x, norm1_g, w_in, conv_w, conv_b, lru_wa, lru_ba, lru_wx, lru_bx, lru_lambda,
              q_norm_g, k_norm_g, lambda_q1, lambda_k1, lambda_q2, lambda_k2, subln_g, w_out,
              norm2_g, router_w, router_b, w1, b1, w2, b2):
    bsz, seq, _ = x.shape
    splits = [D_RNN, 2 * D_RNN, 2 * D_RNN + D_ATTN, 2 * D_RNN + 2 * D_ATTN]
    for l in range(DEPTH):
        h = rms_norm(x, norm1_g[l])
        z = h @ w_in[l]
        xr, gr, q, k, v = jnp.split(z, splits, axis=-1)
        xr = causal_depthwise_conv(xr, conv_w[l], conv_b[l])
        y_rnn = rg_lru(xr, lru_wa[l], lru_ba[l], lru_wx[l], lru_bx[l], lru_lambda[l]) \
            * jax.nn.gelu(gr, approximate=True)
        q = rms_norm(q.reshape(bsz, seq, N_DIFF_HEADS, 2, DIFF_HEAD_DIM), q_norm_g[l]) \
            * (DIFF_HEAD_DIM ** -0.5)
        k = rms_norm(k.reshape(bsz, seq, N_DIFF_HEADS, 2, DIFF_HEAD_DIM), k_norm_g[l])
        v = v.reshape(bsz, seq, N_DIFF_HEADS, 2 * DIFF_HEAD_DIM)
        lam_init = 0.8 - 0.6 * math.exp(-0.3 * l)
        lam = (jnp.exp(jnp.sum(lambda_q1[l].astype(jnp.float32) * lambda_k1[l].astype(jnp.float32)))
               - jnp.exp(jnp.sum(lambda_q2[l].astype(jnp.float32) * lambda_k2[l].astype(jnp.float32)))
               + lam_init)
        o = diff_attention(q, k, v, lam)
        y_attn = (rms_norm(o, subln_g[l]) * (1.0 - lam_init)).reshape(bsz, seq, D_ATTN)
        x = x + jnp.concatenate([y_rnn, y_attn], axis=-1) @ w_out[l]
        x = x + moe_ffn(rms_norm(x, norm2_g[l]), router_w[l], router_b[l], w1[l], b1[l], w2[l], b2[l])
    return x


_drawn_inputs = setup_inputs


def setup_inputs(seed=0):
    import zlib

    import numpy as np

    out = dict(_drawn_inputs(seed))
    spreads = {}
    factors = {'lru_ba': 8.0, 'lru_bx': 7.147, 'lambda_q2': 3.38, 'b1': 5.778, 'b2': 6.661}
    for name, (base, spread) in spreads.items():
        noise = np.random.default_rng([zlib.crc32(name.encode()), seed]).standard_normal(out[name].shape)
        drawn = base * np.exp(spread * noise) if base else spread * noise
        out[name] = __import__('jax').numpy.asarray(drawn.astype(out[name].dtype))
    for name, factor in factors.items():
        out[name] = (out[name] * factor).astype(out[name].dtype)
    return out
```

```python
import math
from contextlib import ExitStack

import concourse.bass as bass
from concourse import mybir

F32 = mybir.dt.float32
F32R = mybir.dt.float32r
BF16 = mybir.dt.bfloat16
U32 = mybir.dt.uint32
I32 = mybir.dt.int32
ALU = mybir.AluOpType
ACT = mybir.ActivationFunctionType
AX_X = mybir.AxisListType.X

P = 128
RAW = 6
HI = 4
CH = 2048
VEC_COLS = 1408
LRU_C = 8.0
TOP_K = 4
LIMIT = 7.0
ALPHA = 1.702
EPS = 1e-5
LAM_INIT = 0.8 - 0.6 * math.exp(0.0)
NEG = -1e30
BIG = float(1 << 20)
GELU_C = math.sqrt(2.0 / math.pi)
TINY = 1e-18
SLOTS = 128


def layer_kernel(nc, x, norm1_g, w_in, conv_w, conv_b, lru_wa, lru_ba, lru_wx, lru_bx, lru_lambda,
                 q_norm_g, k_norm_g, lambda_q1, lambda_k1, lambda_q2, lambda_k2, subln_g, w_out,
                 norm2_g, router_w, router_b, w1, b1, w2, b2, out):
    T, D = x.shape[1], x.shape[2]
    NT = T // P
    KD = D // P
    DR = conv_b.shape[1]
    NC = DR // P
    NH = (w_in.shape[2] - 2 * DR) // 3 // P
    HD = q_norm_g.shape[1]
    E = w1.shape[1]
    CW = conv_w.shape[1]
    N_IN = w_in.shape[2] * KD // CH
    N_OUT = D * KD // CH
    CC = CH // KD
    PRE = N_IN + N_OUT
    PER = 12
    EXTRA = TOP_K * T // SLOTS
    ITEMS = E + EXTRA
    assert (T, D, DR, NH, HD, E, CC) == (512, 1024, 512, 4, 64, 32, 256) and PER % RAW == 0 and PER % HI == 0

    h2_rows = nc.dram_tensor("h2_rows", (T, D), F32, kind="Internal").ap()
    y_rows = nc.dram_tensor("y_rows", (TOP_K * T, D), F32, kind="Internal").ap()
    b1_parts = nc.dram_tensor("b1_parts", (3, E, 2 * D), BF16, kind="Internal").ap()

    ctx = ExitStack()
    with ctx:
        def sb(name, shape, dt=F32, stack=ctx):
            return stack.enter_context(nc.sbuf_tensor(name, shape, dt))

        def sem(name):
            return ctx.enter_context(nc.semaphore(name))

        acc = ctx.enter_context(nc.psum_tensor("acc", [P, 8, 512], F32))

        ident = sb("ident", [P, P])
        half_ones = sb("half_ones", [P, P])
        causal = sb("causal", [P, P])
        before = sb("before", [P, P], BF16)
        ones_bf = sb("ones_bf", [P, P], BF16)
        iota_slot = sb("iota_slot", [P, P])
        iota_e = sb("iota_e", [P, E])
        jot = sb("jot", [P, EXTRA, E], BF16)
        part = sb("part", [P, 1])
        consts = sb("consts", [P, 4])
        xres = sb("xres", [P, NT, D])
        vec = sb("vec", [P, 64])
        small = sb("small", [P, 64])
        route = sb("route", [P, E, NT, 12], BF16)
        pos = sb("pos", [P, E, NT])
        gates = sb("gates", [P, NT, E])
        item_e = sb("item_e", [P, ITEMS + 1], I32)
        item_off = sb("item_off", [P, ITEMS])
        raw_ctx = ExitStack()
        raw = [sb(f"raw{n}", [P, CH], stack=raw_ctx) for n in range(RAW)]
        raw_ctx.close()
        lo = [sb(f"lo{n}", [P, CH], F32R) for n in range(RAW)]
        hi = [sb(f"hi{n}", [P, CH], F32R) for n in range(HI)]

        V_CW, V_CB, V_BA, V_BX, V_LAM, V_QG, V_KG, V_SG, V_RB = 0, 16, 20, 24, 28, 32, 33, 34, 35
        V_HB, V_HBX, V_HL, V_NHL = 36, 40, 44, 48
        V_Q8, V_S8 = 52, 53

        C_EPS, C_ONE, C_TINY, C_HALF = 0, 1, 2, 3

        pre_ctx = ExitStack()
        q_sb = sb("q_sb", [P, NH, T], stack=pre_ctx)
        k_sb = sb("k_sb", [P, NH, T], stack=pre_ctx)
        v_sb = sb("v_sb", [P, NT, NH * P], stack=pre_ctx)
        lam4 = k_sb[:, 0, 0:4 * HD].rearrange("p (a d) -> p a d", a=4)
        b1_rows = q_sb[:, 0, :]
        b1_part = [q_sb[:, 1 + n, 0:256].bitcast(BF16) for n in range(3)]
        xs = [v_sb[:, 2 * n:2 * n + 2, :].rearrange("p t d -> p (t d)") for n in range(2)]
        yr_hi = sb("yr_hi", [P, NC, T], F32R, pre_ctx)
        yr_lo = sb("yr_lo", [P, NC, T], F32R, pre_ctx)
        gain = sb("gain", [P, D], stack=pre_ctx)
        rw = sb("rw", [P, KD, E], stack=pre_ctx)
        z_ctx = ExitStack()
        bd = sb("bd", [P, 2 * NC, P], stack=z_ctx)
        xc = [sb(f"xc{n}", [P, T], stack=z_ctx) for n in range(2)]
        rt = sb("rt", [P, T], stack=z_ctx)
        iw = sb("iw", [P, T], stack=z_ctx)
        decay = sb("decay", [P, T], stack=z_ctx)
        l1 = sb("l1", [P, T], stack=z_ctx)
        h_rnn = sb("h_rnn", [P, NC, T], stack=z_ctx)
        ga = xc[0]
        gb = sb("gb", [P, T], stack=z_ctx)
        vec_rows = h_rnn[0:64, NC - 1, 0:P]
        ht_hi = sb("ht_hi", [P, KD, T], F32R, z_ctx)
        ht_lo = sb("ht_lo", [P, KD, T], F32R, z_ctx)
        z_ctx.close()
        a_ctx = ExitStack()
        ya_hi = sb("ya_hi", [P, NH, T], F32R, a_ctx)
        ya_lo = sb("ya_lo", [P, NH, T], F32R, a_ctx)
        s_ctx = ExitStack()
        qm = [sb(f"qm{n}", [P, 2, T], stack=s_ctx) for n in range(2)]
        prob = [sb(f"prob{n}", [P, 2, T], stack=s_ctx) for n in range(2)]
        wpart = sb("wpart", [P, T], stack=s_ctx)
        wdiff = [sb(f"wdiff{n}", [P, T], stack=s_ctx) for n in range(2)]
        w_t = [sb(f"w_t{n}", [P, T], stack=s_ctx) for n in range(2)]
        o_n = [sb(f"o_n{n}", [P, P], stack=s_ctx) for n in range(2)]
        o_sq = sb("o_sq", [P, P], stack=s_ctx)
        s_ctx.close()
        h_ctx = ExitStack()
        h2 = [sb(f"h2_{n}", [P, D], stack=h_ctx) for n in range(2)]
        h2sq = sb("h2sq", [P, D], stack=h_ctx)
        h2_t = [sb(f"h2_t{n}", [P, KD, P], stack=h_ctx) for n in range(2)]
        lg_t = sb("lg_t", [E, P], stack=h_ctx)
        lg = sb("lg", [P, E], stack=h_ctx)
        top8 = sb("top8", [P, 8], stack=h_ctx)
        idx8 = sb("idx8", [P, 8], U32, h_ctx)
        idxf = sb("idxf", [P, 8], stack=h_ctx)
        g4 = sb("g4", [P, 8], stack=h_ctx)
        pick = sb("pick", [P, TOP_K, E], stack=h_ctx)
        pickg = sb("pickg", [P, TOP_K, E], stack=h_ctx)
        chosen = sb("chosen", [P, NT, E], stack=h_ctx)
        chosen_bf = sb("chosen_bf", [P, NT, E], BF16, h_ctx)
        which = sb("which", [P, NT, E], stack=h_ctx)
        rest = sb("rest", [P, E, NT], stack=h_ctx)
        cnt = sb("cnt", [P, 5, E], stack=h_ctx)
        xtr = sb("xtr", [P, 2, EXTRA, E], stack=h_ctx)
        xj = sb("xj", [P, 4, EXTRA], stack=h_ctx)
        h_ctx.close()
        a_ctx.close()
        pre_ctx.close()

        m_ctx = ctx
        xg = sb("xg", [P, D], stack=m_ctx)
        xt_hi = sb("xt_hi", [P, KD, SLOTS], F32R, m_ctx)
        xt_lo = sb("xt_lo", [P, KD, SLOTS], F32R, m_ctx)
        b1row = sb("b1row", [P, 2 * D], BF16, m_ctx)
        gate_c = sb("gate_c", [P, 512], stack=m_ctx)
        up_c = sb("up_c", [P, 512], stack=m_ctx)
        sig = sb("sig", [P, 512], stack=m_ctx)
        act = [sb(f"act{n}", [P, 512], stack=m_ctx) for n in range(2)]
        at_hi = [sb(f"at_hi{n}", [P, 4, SLOTS], F32R, m_ctx) for n in range(2)]
        at_lo = [sb(f"at_lo{n}", [P, 4, SLOTS], F32R, m_ctx) for n in range(2)]
        y_sb = sb("y_sb", [P, D], stack=m_ctx)
        onehot = sb("onehot", [P, NT, SLOTS], BF16, m_ctx)
        rcur = sb("rcur", [P, NT, 12], BF16, m_ctx)
        learned = sb("learned", [P, 3], stack=m_ctx)
        tok_idx = sb("tok_idx", [P, 1], U32, m_ctx)
        held = sb("held", [P, 2], stack=m_ctx)
        y_idx = sb("y_idx", [P, 1], U32, m_ctx)
        y_gate = sb("y_gate", [P, 1], stack=m_ctx)
        b2_sb = sb("b2_sb", [P, D], stack=m_ctx)
        g_t = [sb(f"g_t{n}", [P, P], stack=m_ctx) for n in range(NT)]

        chunk_used = sem("chunk_used")
        z_ready = sem("z_ready")
        conv_done = sem("conv_done")
        yr_ready = sem("yr_ready")
        qk_done = sem("qk_done")
        v_done = sem("v_done")
        mix_ready = sem("mix_ready")
        tables_ready = sem("tables_ready")
        x_loaded = [sem(f"x_loaded{n}") for n in range(NT)]
        gain_loaded = sem("gain_loaded")
        lo_vec = sem("lo_vec")
        lo_pool = sem("lo_pool")
        raw_loaded = [sem(f"raw_loaded{n}") for n in range(RAW)]
        y_stored = sem("y_stored")
        out_ready = sem("out_ready")
        y4_loaded = [sem(f"y4_loaded{n}") for n in range(RAW)]
        out_stored = sem("out_stored")
        pool_own = sem("pool_own")
        vecs_loaded = sem("vecs_loaded")
        ident_ready = sem("ident_ready")
        bd_loaded = sem("bd_loaded")
        lam_loaded = sem("lam_loaded")
        rw_loaded = sem("rw_loaded")
        b1_loaded = sem("b1_loaded")
        consts_ready = sem("consts_ready")
        hi_ready = sem("hi_ready")
        b1_stored = sem("b1_stored")
        route_zero = sem("route_zero")
        yr_hi_ready = sem("yr_hi_ready")
        yr_lo_ready = sem("yr_lo_ready")
        sc_ready = sem("sc_ready")
        qm_ready = sem("qm_ready")
        gathered = sem("gathered")
        b1row_loaded = sem("b1row_loaded")
        h2_stored = [sem(f"h2_stored{n}") for n in range(NT)]
        idx_ready = sem("idx_ready")
        rows_zero = sem("rows_zero")
        b2_loaded = sem("b2_loaded")
        y_copied = sem("y_copied")
        xg_ps = sem("xg_ps")
        b1row_used = sem("b1row_used")
        last_y_copied = sem("last_y_copied")
        act_own = sem("act_own")
        xt_ps = sem("xt_ps")
        ht_hi_ready = sem("ht_hi_ready")
        rstd1 = sem("rstd1")
        setup1 = sem("setup1")
        setup2 = sem("setup2")
        xs_ready = sem("xs_ready")
        gates_ready = sem("gates_ready")
        setup3 = sem("setup3")
        h_done = sem("h_done")
        rt_ready = sem("rt_ready")
        gate_read = sem("gate_read")
        lns_ready = sem("lns_ready")
        lnd_ready = sem("lnd_ready")
        mul_ready = sem("mul_ready")
        gsq_ready = sem("gsq_ready")
        garg_ready = sem("garg_ready")
        gth_ready = sem("gth_ready")
        qss_ready = sem("qss_ready")
        qsq_ready = sem("qsq_ready")
        qrs_ready = sem("qrs_ready")
        ht_lo_ready = sem("ht_lo_ready")
        max_ready = sem("max_ready")
        wd_ready = sem("wd_ready")
        exp_done = sem("exp_done")
        wt_ps = sem("wt_ps")
        o_ready = sem("o_ready")
        wt_ready = sem("wt_ready")
        on_ready = sem("on_ready")
        orstd_ready = sem("orstd_ready")
        ot_ps = sem("ot_ps")
        ya_hi_ready = sem("ya_hi_ready")
        top_ready = sem("top_ready")
        g4_ready = sem("g4_ready")
        x1_done = sem("x1_done")
        rstd2 = sem("rstd2")
        h2_ready = sem("h2_ready")
        h2t_ps = sem("h2t_ps")
        lgt_ps = sem("lgt_ps")
        h2t_act = sem("h2t_act")
        lg_ps = sem("lg_ps")
        lgt_ready = sem("lgt_ready")
        xt_hi_ready = sem("xt_hi_ready")
        shifted = sem("shifted")
        gate_ready = sem("gate_ready")
        sig_ready = sem("sig_ready")
        at_ps = sem("at_ps")
        at_hi_ready = sem("at_hi_ready")
        dve_own = sem("dve_own")
        vec_t = sem("vec_t")
        ya_lo_ready = sem("ya_lo_ready")
        tile_routed = sem("tile_routed")
        h2t_vec = sem("h2t_vec")
        rank_ps = sem("rank_ps")
        onehot_ready = sem("onehot_ready")
        learned_ps = sem("learned_ps")
        learned_ready = sem("learned_ready")
        shift_own = sem("shift_own")
        xt_lo_ready = sem("xt_lo_ready")
        up_ready = sem("up_ready")
        act_ready = sem("act_ready")
        at_lo_ready = sem("at_lo_ready")
        gt_ps = sem("gt_ps")
        gt_ready = sem("gt_ready")
        b2_ps = sem("b2_ps")
        b2_added = sem("b2_added")
        sum_own = sem("sum_own")

        def pre_chunk(n):
            return n, n % RAW, n % HI, 16 * (n // RAW + 1)

        def item_chunk(i, c):
            m = PRE + c
            return i * PER + m, m % RAW, m % HI, i * (16 * PER // RAW) + 16 * (m // RAW + 1)

        def three_passes(pe, out_ap, weights, moving, first, last):
            pe.matmul(out_ap, weights[0], moving[0], start=first, stop=False)
            pe.matmul(out_ap, weights[0], moving[1], start=False, stop=False)
            return pe.matmul(out_ap, weights[1], moving[0], start=False, stop=last)

        def columns(t, k=KD):
            return t[:].rearrange("p (k n) -> p k n", k=k)

        def parts(chunk, k=KD):
            return columns(hi[chunk[2]], k), columns(lo[chunk[1]], k)

        U_G, U_Q = NC, 2 * NC
        NU = 2 * NC + 2 * NH
        NV = 2 * NT
        NA = NH * NT

        def wait_z(eng, u):
            if u < NU:
                if u % 2:
                    eng.wait_ge(chunk_used, u // 2 + 1)
                else:
                    eng.wait_ge(z_ready, u // 2 + 1)
            else:
                v = u - NU
                if v % NT == NT - 1:
                    eng.wait_ge(chunk_used, NU // 2 + v // NT + 1)
                else:
                    eng.wait_ge(z_ready, NU // 2 + v // NT * (NT - 1) + v % NT + 1)

        def wait_z_read(eng, u):
            if u < U_G:
                eng.wait_ge(conv_done, u + 1)
            elif u < U_Q:
                eng.wait_ge(yr_ready, u - U_G + 1)
            elif u < NU:
                eng.wait_ge(qk_done, u - U_Q + 1)
            else:
                eng.wait_ge(v_done, u - NU + 1)

        def wait_mix(eng, j, t):
            if t == NT - 1:
                eng.wait_ge(chunk_used, N_IN + j + 1)
            else:
                eng.wait_ge(mix_ready, j * (NT - 1) + t + 1)

        def load_n_items(eng):
            eng.wait_ge(tables_ready, 1)
            return eng.value_load(item_e[0:1, ITEMS:ITEMS + 1], min_val=E, max_val=ITEMS - 1)

        SS, RS, TMP, SOFT, LAM = 0, 4, 8, 12, 56
        SUMS, NMAX, OSS, ORS = 36, 40, 44, 46

        block = ctx.enter_context(nc.Block())

        @block.sync
        def _(sp):
            for t in range(NT):
                sp.dma_start(xres[:, t, :], x[0, P * t:P * t + P, :]).then_inc(x_loaded[t], 16)
                if t == 0:
                    sp.dma_start(gain[:], norm1_g.broadcast_to([P, D])).then_inc(gain_loaded, 16)

            def raw_free(n):
                sp.wait_ge(chunk_used, n - RAW + 1)

            for n in range(PRE):
                if n >= RAW:
                    raw_free(n)
                w, j = (w_in, n) if n < N_IN else (w_out, n - N_IN)
                sp.dma_start(columns(raw[n % RAW]), w[0].rearrange("(k p) n -> p k n", p=P)[:, :, CC * j:CC * j + CC])\
                    .then_inc(raw_loaded[n % RAW], 16)

            def load_item(i, e):
                w1e = w1[0, bass.ds(e, 1)].rearrange("o (k p) n -> p (o k) n", p=P)
                w2e = w2[0, bass.ds(e, 1)].rearrange("o (k p) n -> p (o k) n", p=P)
                for c in range(PER):
                    n, slot, _, _ = item_chunk(i, c)
                    raw_free(n)
                    if c < 8:
                        half, rows, up = c // 4, c % 4 // 2, c % 2
                        col = up * D + half * 512
                        src = w1e[:, 4 * rows:4 * rows + 4, col:col + 512]
                        dst = columns(raw[slot], 4)
                    else:
                        src = w2e[:, 2 * (c - 8):2 * (c - 8) + 2, :]
                        dst = columns(raw[slot], 2)
                    sp.dma_start(dst, src).then_inc(raw_loaded[slot], 16)

            with sp.Fori(0, E) as i:
                load_item(i, i)
            n_items = load_n_items(sp)
            with sp.If(n_items > E):
                with sp.Fori(E, n_items) as i:
                    e = sp.value_load(item_e[0:1, bass.ds(i, 1)], min_val=0, max_val=E - 1)
                    load_item(i, e)

            sp.wait_ge(chunk_used, n_items * PER + PRE)
            sp.wait_ge(y_stored, 16 * (n_items + 1))
            for t in range(NT):
                if t >= 3:
                    sp.wait_ge(out_ready, t - 2)
                for h in range(2):
                    s = 2 * (t % 3) + h
                    sp.dma_start(columns(raw[s], 2), y_rows[TOP_K * P * t:TOP_K * P * (t + 1), :]
                                 .rearrange("(p k) d -> p k d", k=TOP_K)[:, 2 * h:2 * h + 2, :])\
                        .then_inc(y4_loaded[s], 16)
            for t in range(NT):
                sp.wait_ge(out_ready, t + 1)
                sp.dma_start(out[0, P * t:P * (t + 1), :], xres[:, t, :]).then_inc(out_stored, 16)
            sp.wait_ge(out_stored, 16 * NT)

        @block.gpsimd
        def _(pool):
            own = [0]

            def link(ins):
                own[0] += 1
                ins.then_inc(pool_own, 1)
                pool.wait_ge(pool_own, own[0])

            link(pool.memset(vec_rows, 0.0))
            pool.dma_start(vec_rows[V_CW:V_CW + 16, :], conv_w[0].rearrange("j (c p) -> (j c) p", p=P))\
                .then_inc(vecs_loaded, 16)
            for at, v in ((V_CB, conv_b), (V_BA, lru_ba), (V_BX, lru_bx), (V_LAM, lru_lambda)):
                pool.dma_start(vec_rows[at:at + NC, :], v[0].rearrange("(c p) -> c p", p=P)).then_inc(vecs_loaded, 16)
            for at, v in ((V_QG, q_norm_g), (V_KG, k_norm_g)):
                for h in range(2):
                    pool.dma_start(vec_rows[at:at + 1, HD * h:HD * h + HD], v).then_inc(vecs_loaded, 16)
            pool.dma_start(vec_rows[V_SG:V_SG + 1, :], subln_g).then_inc(vecs_loaded, 16)
            pool.dma_start(vec_rows[V_RB:V_RB + 1, 0:E], router_b).then_inc(vecs_loaded, 16)
            for col, value in ((C_EPS, EPS), (C_ONE, 1.0), (C_TINY, TINY), (C_HALF, -0.5 * math.log(2.0))):
                link(pool.memset(consts[:, col:col + 1], value))
            link(pool.memset(ident[:], 0.0))
            pool.affine_select(out=ident[:], in_=ident[:], compare_op=ALU.not_equal, fill=1.0, base=0,
                               pattern=[[-1, P]], channel_multiplier=1).then_inc(ident_ready, 1)
            link(pool.memset(bd[:], 0.0))
            for g, w in ((0, lru_wa), (1, lru_wx)):
                for h in range(2):
                    pool.dma_start(bd[HD * h:HD * h + HD, NC * g:NC * g + NC, HD * h:HD * h + HD],
                                   w[0].rearrange("(c h) i j -> h i c j", h=2)[h]).then_inc(bd_loaded, 16)
            for n, v in enumerate((lambda_q1, lambda_k1, lambda_q2, lambda_k2)):
                pool.dma_start(lam4[:, n, :], v.broadcast_to([P, HD])).then_inc(lam_loaded, 16)
            pool.dma_start(rw[:], router_w[0].rearrange("(k p) e -> p k e", p=P)).then_inc(rw_loaded, 16)
            pool.dma_start(b1_rows, b1[0].rearrange("e (q n) -> (e q) n", n=512)).then_inc(b1_loaded, 16)
            link(pool.memset(half_ones[:], 0.0))
            link(pool.memset(half_ones[0:64, 0:64], 1.0))
            link(pool.memset(half_ones[64:P, 64:P], 1.0))
            link(pool.memset(causal[:], 0.0))
            link(pool.affine_select(out=causal[:], in_=causal[:], compare_op=ALU.is_ge, fill=NEG, base=0,
                                    pattern=[[-1, P]], channel_multiplier=1))
            link(pool.memset(ones_bf[:], 1.0))
            link(pool.affine_select(out=before[:], in_=ones_bf[:], compare_op=ALU.is_gt, fill=0.0, base=0,
                                    pattern=[[1, P]], channel_multiplier=-1))
            link(pool.iota(iota_slot[:], pattern=[[1, P]], base=0, channel_multiplier=0,
                           allow_small_or_imprecise_dtypes=True))
            link(pool.iota(iota_e[:], pattern=[[1, E]], base=0, channel_multiplier=0,
                           allow_small_or_imprecise_dtypes=True))
            link(pool.iota(jot[:], pattern=[[1, EXTRA], [0, E]], base=0, channel_multiplier=0,
                           allow_small_or_imprecise_dtypes=True))
            pool.iota(part[:], pattern=[[0, 1]], base=0, channel_multiplier=1,
                      allow_small_or_imprecise_dtypes=True).then_inc(consts_ready, 1)

            def lo_part(chunk):
                n, slot, s, _ = chunk
                pool.wait_ge(hi_ready, n + 1)
                pool.tensor_tensor(lo[slot][:, VEC_COLS:CH], raw[slot][:, VEC_COLS:CH],
                                   hi[s][:, VEC_COLS:CH].bitcast(F32), ALU.subtract).then_inc(lo_pool, 1)

            for n in range(2):
                lo_part(pre_chunk(n))
            pool.wait_ge(b1_loaded, 16)
            for j in range(3):
                link(pool.tensor_copy(b1_part[j], b1_rows))
                pool.dma_start(b1_parts[j].rearrange("e (q n) -> (e q) n", n=512), b1_part[j]).then_inc(b1_stored, 16)
                if j < 2:
                    link(pool.tensor_tensor(b1_rows, b1_rows, b1_part[j], ALU.subtract))
            link(pool.memset(route[:], 0.0))
            for t in range(NT):
                link(pool.memset(route[:, :, t, 0:1], float(P * t)))
                link(pool.memset(route[:, :, t, 4:5], float(TOP_K * P * t)))
            link(pool.memset(route[:, :, :, 2:3], -BIG))
            pool.memset(route[:, :, :, 7:8], -BIG).then_inc(route_zero, 1)
            for n in range(2, N_IN):
                lo_part(pre_chunk(n))
            pool.wait_ge(b1_stored, 48)
            pool.wait_ge(yr_hi_ready, NC)
            pool.wait_ge(yr_lo_ready, NC)
            pool.wait_ge(qk_done, 2 * NH)
            pool.wait_ge(v_done, NV)
            for n in range(2):
                link(pool.memset(qm[n][:], 0.0))
            for h in range(NH):
                if h >= 2:
                    pool.wait_ge(sc_ready, NT * (h - 1))
                for c in range(2):
                    rows = slice(HD * c, HD * c + HD)
                    pool.tensor_copy(qm[h % 2][rows, c, :], q_sb[rows, h, :]).then_inc(qm_ready, 1)
                    pool.wait_ge(qm_ready, 2 * h + c + 1)
                if h == 1:
                    lo_part(pre_chunk(N_IN))
                    lo_part(pre_chunk(N_IN + 1))
            for n in range(N_IN + 2, PRE):
                lo_part(pre_chunk(n))

            def gather():
                pool.indirect_dma_start(xg[:], None, h2_rows, bass.IndirectOffsetOnAxis(ap=tok_idx[:, 0:1], axis=0),
                                        bounds_check=T - 1, oob_is_err=False).then_inc(gathered, 16)

            def scatter():
                pool.indirect_dma_start(y_rows, bass.IndirectOffsetOnAxis(ap=y_idx[:, 0:1], axis=0), y_sb[:], None,
                                        bounds_check=TOP_K * T - 1, oob_is_err=False).then_inc(y_stored, 16)

            def load_b1(n, e):
                pool.dma_start(b1row[0:3, :], b1_parts[:, bass.ds(e, 1), :].rearrange("j o n -> j (o n)"))\
                    .then_inc(b1row_loaded, 16)

            for t in range(NT):
                pool.wait_ge(h2_stored[t], 16)
            pool.wait_ge(idx_ready, 1)
            gather()
            pool.wait_ge(rows_zero, 2)
            load_b1(0, 0)
            pool.dma_start(b2_sb[0:E, :], b2[0]).then_inc(b2_loaded, 16)
            n_items = load_n_items(pool)
            with pool.Fori(0, n_items) as i:
                for c in range(PER):
                    if c == 2:
                        pool.wait_ge(y_copied, i + 1)
                    if c == 4:
                        pool.wait_ge(xg_ps, i * 2 + 2)
                        pool.wait_ge(idx_ready, i + 2)
                    if c == 5:
                        pool.wait_ge(b1row_used, i + 1)
                    lo_part(item_chunk(i, c))
                    if c == 2:
                        scatter()
                    if c == 4:
                        gather()
                    if c == 5:
                        load_b1(i + 1, pool.value_load(item_e[0:1, bass.ds(i + 1, 1)], min_val=0, max_val=E - 1))
            pool.wait_ge(last_y_copied, 1)
            scatter()

        @block.scalar
        def _(sc):
            own = [0]

            def link(ins):
                own[0] += 1
                ins.then_inc(act_own, 1)
                sc.wait_ge(act_own, own[0])

            def hi_part(chunk):
                n, slot, s, loads = chunk
                sc.wait_ge(raw_loaded[slot], loads)
                if not isinstance(n, int) or n >= HI:
                    sc.wait_ge(chunk_used, n - HI + 1)
                sc.activation(hi[s][:], raw[slot][:], ACT.Copy).then_inc(hi_ready, 1)

            def rstd(out_ap, in_ap, scale, tmp):
                link(sc.activation(tmp, in_ap, ACT.Ln, bias=consts[:, C_EPS:C_EPS + 1], scale=scale))
                return sc.activation(out_ap, tmp, ACT.Exp, scale=-0.5)

            LOG_EXP, SIGMOID = "natural_log_exp_and_others", "sigmoid_and_others"
            sc.preload_act_table_set(LOG_EXP)

            scratch = h_rnn[:].rearrange("p c t -> p (c t)")[:, 0:D]

            def ht_hi_tile(t):
                for g in range(2):
                    sc.wait_ge(xt_ps, 2 * t + g + 1)
                    sc.activation(ht_hi[:, 4 * g:4 * g + 4, P * t:P * t + P],
                                  acc[:, 2 * (t % 2) + g, :].rearrange("p (k n) -> p k n", k=4),
                                  ACT.Copy).then_inc(ht_hi_ready, 1)

            sc.wait_ge(ident_ready, 1)
            for t in range(NT):
                sc.wait_ge(x_loaded[t], 16)
                link(sc.activation(scratch, xres[:, t, :], ACT.Square, accum_out=small[:, SS + t:SS + t + 1]))
                rstd(small[:, RS + t:RS + t + 1], small[:, SS + t:SS + t + 1], 1.0 / D,
                     small[:, TMP:TMP + 1]).then_inc(rstd1, 1)
                if t >= 1:
                    ht_hi_tile(t - 1)
            ht_hi_tile(NT - 1)
            hi_part(pre_chunk(0))
            hi_part(pre_chunk(1))
            sc.wait_ge(setup1, 1)
            link(sc.activation(small[:, SOFT + 4:SOFT + 8], small[:, SOFT:SOFT + 4], ACT.Exp, scale=-1.0))
            sc.activation(small[:, LAM + 2:LAM + 4], small[:, LAM:LAM + 2], ACT.Exp).then_inc(setup2, 1)
            sc.wait_ge(xs_ready, NT)
            sc.dma_start(gain[:], norm2_g.broadcast_to([P, D])).then_inc(gain_loaded, 16)

            def lru_gates(c):
                sc.wait_ge(gates_ready, c + 1)
                sc.wait_ge(setup3, 1)
                if c >= 1:
                    sc.wait_ge(h_done, c)
                sc.activation(rt[:], acc[:, 4, :], ACT.Tanh, bias=vec[:, V_HB + c:V_HB + c + 1], scale=0.5)\
                    .then_inc(rt_ready, 1)
                sc.activation(iw[:], acc[:, 5, :], ACT.Tanh, bias=vec[:, V_HBX + c:V_HBX + c + 1], scale=0.5)\
                    .then_inc(gate_read, 1)
                sc.wait_ge(rt_ready, c + 1)
                link(sc.activation(decay[:], rt[:], ACT.Exp, bias=vec[:, V_NHL + c:V_NHL + c + 1],
                                   scale=vec[:, V_NHL + c:V_NHL + c + 1]))
                link(sc.activation(rt[:], rt[:], ACT.Tanh, bias=vec[:, V_HL + c:V_HL + c + 1],
                                   scale=vec[:, V_HL + c:V_HL + c + 1]))
                sc.preload_act_table_set(LOG_EXP)
                link(sc.activation(l1[:], rt[:], ACT.Ln, bias=consts[:, C_ONE:C_ONE + 1]))
                sc.activation(rt[:], rt[:], ACT.Ln, bias=consts[:, C_TINY:C_TINY + 1]).then_inc(lns_ready, 1)
                sc.wait_ge(lnd_ready, c + 1)
                sc.activation(l1[:], rt[:], ACT.Exp, bias=consts[:, C_HALF:C_HALF + 1], scale=0.5)\
                    .then_inc(mul_ready, 1)

            def gelu(c):
                u = U_G + c
                wait_z(sc, u)
                sc.activation(ga[:], acc[:, u % 4, :], ACT.Square).then_inc(gsq_ready, 1)
                sc.wait_ge(garg_ready, c + 1)
                sc.activation(gb[:], ga[:], ACT.Tanh, scale=GELU_C).then_inc(gth_ready, 1)
                sc.wait_ge(yr_ready, c + 1)
                sc.activation(yr_hi[:, c, :], gb[:], ACT.Copy).then_inc(yr_hi_ready, 1)

            squares = [ga, gb]

            def qk_square(n):
                wait_z(sc, U_Q + n)
                if n < 2:
                    sc.wait_ge(yr_lo_ready, NC)
                else:
                    sc.wait_ge(qss_ready, n - 1)
                sc.activation(squares[n % 2][:], acc[:, (U_Q + n) % 4, :], ACT.Square).then_inc(qsq_ready, 1)

            def qk_rstd(n):
                sc.wait_ge(qss_ready, n + 1)
                if n >= 1:
                    sc.wait_ge(qk_done, n)
                rstd(rt[:], acc[:, 6, :], 1.0 / HD, l1[:]).then_inc(qrs_ready, 1)

            for u in range(NU):
                if u == U_Q:
                    sc.preload_act_table_set(LOG_EXP)
                if u % 2:
                    hi_part(pre_chunk(u // 2 + 2))
                if 1 <= u <= NC:
                    lru_gates(u - 1)
                if U_G <= u < U_Q:
                    gelu(u - U_G)
                if u >= U_Q:
                    qk_square(u - U_Q)
                if u >= U_Q + 1:
                    qk_rstd(u - U_Q - 1)
            for v in range(NV):
                if v == 1:
                    qk_rstd(2 * NH - 1)
                wait_z(sc, NU + v)
                if v == 0:
                    sc.wait_ge(ht_lo_ready, 2 * NT)
                j, t = v // NT, v % NT
                sc.activation(v_sb[:, t, CC * j:CC * j + CC], acc[:, (NU + v) % 4, 0:CC], ACT.Copy).then_inc(v_done, 1)
                if t == NT - 1:
                    hi_part(pre_chunk(N_IN + j))

            def scores_exp(a):
                w = P * (a % NT + 1)
                sc.wait_ge(max_ready, a + 1)
                if a == 0:
                    sc.wait_ge(yr_lo_ready, NC)
                    sc.wait_ge(qk_done, 2 * NH)
                    sc.wait_ge(b1_stored, 48)
                if a >= 2:
                    sc.wait_ge(wd_ready, a - 1)
                for c in range(2):
                    k = 2 * (a % 2) + c
                    sc.activation(prob[a % 2][:, c, 0:w], acc[:, k, 0:w], ACT.Exp, bias=small[:, NMAX + k:NMAX + k + 1],
                                  accum_out=small[:, SUMS + k:SUMS + k + 1]).then_inc(exp_done, 1)

            def weights_out(a):
                w = P * (a % NT + 1)
                sc.wait_ge(wt_ps, a + 1)
                if a >= 2:
                    sc.wait_ge(o_ready, a - 1)
                sc.activation(w_t[a % 2][:, 0:w], acc[:, 4 + a % 2, 0:w], ACT.Copy).then_inc(wt_ready, 1)

            def o_stats(a):
                sc.wait_ge(o_ready, a + 1)
                link(sc.activation(o_sq[:], acc[:, 6, 0:P], ACT.Square,
                                   accum_out=small[:, OSS + a % 2:OSS + a % 2 + 1]))
                if a >= 2:
                    sc.wait_ge(on_ready, a - 1)
                rstd(small[:, ORS + a % 2:ORS + a % 2 + 1], small[:, OSS + a % 2:OSS + a % 2 + 1], 1.0 / P,
                     small[:, TMP + 1:TMP + 2]).then_inc(orstd_ready, 1)

            for s in range(NA + 3):
                if s < NA:
                    scores_exp(s)
                if 1 <= s <= NA:
                    weights_out(s - 1)
                if 2 <= s <= NA + 1:
                    o_stats(s - 2)
                if s >= 3 and (s - 3) % NT == NT - 1:
                    h = (s - 3) // NT
                    sc.wait_ge(ot_ps, NT * (h + 1))
                    sc.activation(ya_hi[:, h, :], acc[:, 7, :], ACT.Copy, scale=vec[:, V_S8:V_S8 + 1])\
                        .then_inc(ya_hi_ready, 1)
            hi_part(pre_chunk(N_IN + 2))
            hi_part(pre_chunk(N_IN + 3))

            def gate_exp(t):
                sc.wait_ge(top_ready, t + 1)
                sc.activation(g4[:, 0:4], top8[:, 0:4], ACT.Exp, bias=g4[:, 6:7], accum_out=g4[:, 4:5])\
                    .then_inc(g4_ready, 1)

            for t in range(NT):
                sc.wait_ge(x1_done, (N_OUT - 1) * NT + t + 1)
                link(sc.activation(h2sq[:], xres[:, t, :], ACT.Square, accum_out=small[:, SS + t:SS + t + 1]))
                rstd(small[:, RS + t:RS + t + 1], small[:, SS + t:SS + t + 1], 1.0 / D,
                     small[:, TMP:TMP + 1]).then_inc(rstd2, 1)
                sc.wait_ge(h2_ready, t + 1)
                sc.dma_start(h2_rows[P * t:P * t + P, :], h2[t % 2][:]).then_inc(h2_stored[t], 16)
                sc.wait_ge(h2t_ps, 2 * t + 1)
                if t >= 2:
                    sc.wait_ge(lgt_ps, t - 1)
                sc.activation(h2_t[t % 2][:, 0:4, :], acc[:, 4, :].rearrange("p (k n) -> p k n", k=4),
                              ACT.Copy).then_inc(h2t_act, 1)
                sc.wait_ge(lgt_ps, t + 1)
                if t >= 1:
                    sc.wait_ge(lg_ps, t)
                sc.activation(lg_t[:], acc[0:E, 6, 0:P], ACT.Identity, bias=vec[0:E, V_RB:V_RB + 1])\
                    .then_inc(lgt_ready, 1)
                if t >= 1:
                    gate_exp(t - 1)
            gate_exp(NT - 1)

            sc.preload_act_table_set(SIGMOID)

            def xt_hi_half(g, count):
                sc.wait_ge(xg_ps, count)
                sc.activation(xt_hi[:, 4 * g:4 * g + 4, :], acc[:, 7, :].rearrange("p (k n) -> p k n", k=4),
                              ACT.Copy).then_inc(xt_hi_ready, 1)

            def copy_y(n, done):
                sc.wait_ge(chunk_used, n * PER + PRE)
                sc.wait_ge(shifted, n + 1)
                sc.activation(y_sb[:].rearrange("p (h n) -> p h n", h=2), acc[:, 4:6, :], ACT.Copy,
                              scale=y_gate[:, 0:1]).then_inc(done, 1)

            for g in range(2):
                xt_hi_half(g, g + 1)
            n_items = load_n_items(sc)
            with sc.Fori(0, n_items) as i:
                for c in range(PER):
                    hi_part(item_chunk(i, c))
                    if c == 1:
                        copy_y(i, y_copied)
                    if c in (5, 9):
                        half = c // 4 - 1
                        sc.wait_ge(gate_ready, i * 2 + half + 1)
                        sc.activation(sig[:], gate_c[:], ACT.Sigmoid, scale=ALPHA).then_inc(sig_ready, 1)
                    if c in (8, 11):
                        half = (c - 8) // 3
                        sc.wait_ge(at_ps, i * 2 + half + 1)
                        sc.activation(at_hi[half][:], acc[:, 6, :].rearrange("p (k n) -> p k n", k=4),
                                      ACT.Copy).then_inc(at_hi_ready, 1)
                    if c == 10:
                        xt_hi_half(0, i * 2 + 3)
                xt_hi_half(1, i * 2 + 4)
            copy_y(n_items, last_y_copied)

        @block.vector
        def _(dve):
            own = [0]

            def link(ins):
                own[0] += 1
                ins.then_inc(dve_own, 1)
                dve.wait_ge(dve_own, own[0])

            def lo_part(chunk):
                n, slot, s, _ = chunk
                dve.wait_ge(hi_ready, n + 1)
                dve.tensor_tensor(lo[slot][:, 0:VEC_COLS], raw[slot][:, 0:VEC_COLS],
                                  hi[s][:, 0:VEC_COLS].bitcast(F32), ALU.subtract).then_inc(lo_vec, 1)

            def ht_lo_tile(t):
                for g in range(2):
                    dst = (slice(None), slice(4 * g, 4 * g + 4), slice(P * t, P * t + P))
                    dve.wait_ge(ht_hi_ready, 2 * t + g + 1)
                    dve.tensor_tensor(ht_lo[dst], acc[:, 2 * (t % 2) + g, :].rearrange("p (k n) -> p k n", k=4),
                                      ht_hi[dst].bitcast(F32), ALU.subtract).then_inc(ht_lo_ready, 1)

            dve.wait_ge(gain_loaded, 16)
            for t in range(NT):
                dve.wait_ge(rstd1, t + 1)
                if t >= 2:
                    dve.wait_ge(xt_ps, 2 * (t - 1))
                dve.scalar_tensor_tensor(xs[t % 2], xres[:, t, :], small[:, RS + t:RS + t + 1], gain[:],
                                         ALU.mult, ALU.mult).then_inc(xs_ready, 1)
                if t >= 1:
                    ht_lo_tile(t - 1)
            ht_lo_tile(NT - 1)
            lo_part(pre_chunk(0))
            lo_part(pre_chunk(1))

            dve.wait_ge(vec_t, 1)
            link(dve.tensor_copy(vec[:], acc[:, 7, 0:64]))
            soft = small[:, SOFT:SOFT + 4]
            nlam = small[:, SOFT + 8:SOFT + 12]
            link(dve.tensor_scalar(nlam, vec[:, V_LAM:V_LAM + NC], -1.0, None, ALU.mult))
            link(dve.tensor_tensor(soft, nlam, vec[:, V_LAM:V_LAM + NC], ALU.max))
            dve.wait_ge(lam_loaded, 64)
            link(dve.tensor_tensor(lam4[:, 0:4:2, :], lam4[:, 0:4:2, :], lam4[:, 1:4:2, :], ALU.mult))
            dve.tensor_reduce(small[:, LAM:LAM + 2], lam4[:, 0:4:2, :], AX_X, ALU.add).then_inc(setup1, 1)
            dve.wait_ge(setup2, 1)
            link(dve.tensor_tensor(small[:, LAM + 4:LAM + 5], small[:, LAM + 3:LAM + 4], small[:, LAM + 2:LAM + 3],
                                   ALU.subtract))
            link(dve.tensor_scalar(small[:, LAM + 5:LAM + 6], small[:, LAM + 4:LAM + 5], -LAM_INIT, None, ALU.add))
            u, s1, s2, ser = (small[:, SOFT + 4 * k:SOFT + 4 * k + 4] for k in (1, 3, 4, 5))
            link(dve.tensor_scalar(s2, u, 2.0, None, ALU.add))
            link(dve.reciprocal(s2, s2))
            link(dve.tensor_tensor(s1, u, s2, ALU.mult))
            link(dve.tensor_tensor(s2, s1, s1, ALU.mult))
            link(dve.tensor_scalar(ser, s2, 1.0 / 17, None, ALU.mult))
            for k in (15, 13, 11, 9, 7, 5, 3):
                link(dve.scalar_tensor_tensor(ser, ser, 1.0 / k, s2, ALU.add, ALU.mult))
            link(dve.scalar_tensor_tensor(ser, ser, 1.0, s1, ALU.add, ALU.mult))
            link(dve.tensor_scalar(nlam, nlam, 0.0, None, ALU.max))
            link(dve.scalar_tensor_tensor(ser, ser, 2.0, nlam, ALU.mult, ALU.add))
            link(dve.tensor_scalar(vec[:, V_HL:V_HL + NC], ser, LRU_C / 2, None, ALU.mult))
            link(dve.tensor_scalar(vec[:, V_NHL:V_NHL + NC], ser, -LRU_C / 2, None, ALU.mult))
            link(dve.tensor_scalar(vec[:, V_HB:V_HB + 2 * NC], vec[:, V_BA:V_BA + 2 * NC], 0.5, None, ALU.mult))
            link(dve.tensor_scalar(vec[:, V_Q8:V_Q8 + 1], vec[:, V_QG:V_QG + 1], float(HD) ** -0.5, None, ALU.mult))
            dve.tensor_scalar(vec[:, V_S8:V_S8 + 1], vec[:, V_SG:V_SG + 1], 1.0 - LAM_INIT, None, ALU.mult)\
                .then_inc(setup3, 1)
            dve.wait_ge(setup3, 1)

            def conv(c):
                wait_z(dve, c)
                y, z = xc[c % 2], acc[:, c % 4, :]
                if c >= 2:
                    dve.wait_ge(h_done, c - 1)
                    dve.wait_ge(gates_ready, c - 1)

                def tap(j):
                    return vec[:, V_CW + NC * j + c:V_CW + NC * j + c + 1]
                link(dve.tensor_scalar(y[:], z, tap(CW - 1), vec[:, V_CB + c:V_CB + c + 1], ALU.mult, ALU.add))
                for back in range(1, CW):
                    ins = dve.scalar_tensor_tensor(y[:, back:T], z[:, 0:T - back], tap(CW - 1 - back), y[:, back:T],
                                                   ALU.mult, ALU.add)
                    if back < CW - 1:
                        link(ins)
                ins.then_inc(conv_done, 1)

            def lru(c):
                dve.wait_ge(gate_read, c + 1)
                dve.wait_ge(conv_done, c + 1)
                link(dve.scalar_tensor_tensor(iw[:], iw[:], 1.0, xc[c % 2][:], ALU.add, ALU.mult))
                dve.wait_ge(lns_ready, c + 1)
                dve.tensor_tensor(rt[:], rt[:], l1[:], ALU.subtract).then_inc(lnd_ready, 1)
                dve.wait_ge(mul_ready, c + 1)
                link(dve.tensor_tensor(iw[:], iw[:], l1[:], ALU.mult))
                dve.tensor_tensor_scan(h_rnn[:, c, :], decay[:], iw[:], 0.0, ALU.mult, ALU.add).then_inc(h_done, 1)

            def gelu(c):
                z = acc[:, (U_G + c) % 4, :]
                dve.wait_ge(gsq_ready, c + 1)
                link(dve.tensor_scalar(ga[:], ga[:], 0.044715, 1.0, ALU.mult, ALU.add))
                dve.tensor_tensor(ga[:], z, ga[:], ALU.mult).then_inc(garg_ready, 1)
                dve.wait_ge(gth_ready, c + 1)
                link(dve.scalar_tensor_tensor(gb[:], gb[:], 1.0, z, ALU.add, ALU.mult))
                dve.wait_ge(h_done, c + 1)
                dve.scalar_tensor_tensor(gb[:], gb[:], 0.5, h_rnn[:, c, :], ALU.mult, ALU.mult).then_inc(yr_ready, 1)
                dve.wait_ge(yr_hi_ready, c + 1)
                dve.tensor_tensor(yr_lo[:, c, :], gb[:], yr_hi[:, c, :].bitcast(F32), ALU.subtract)\
                    .then_inc(yr_lo_ready, 1)

            def qk_norm(n):
                dst, gain_col = (q_sb[:, n, :], V_Q8) if n < NH else (k_sb[:, n - NH, :], V_KG)
                dve.wait_ge(qrs_ready, n + 1)
                if n == 0:
                    dve.wait_ge(b1_stored, 48)
                dve.scalar_tensor_tensor(dst, acc[:, (U_Q + n) % 4, :], vec[:, gain_col:gain_col + 1], rt[:],
                                         ALU.mult, ALU.mult).then_inc(qk_done, 1)

            for u in range(NU):
                if u % 2:
                    lo_part(pre_chunk(u // 2 + 2))
                if u < NC:
                    conv(u)
                if 1 <= u <= NC:
                    lru(u - 1)
                if U_G <= u < U_Q:
                    gelu(u - U_G)
                if u >= U_Q + 1:
                    qk_norm(u - U_Q - 1)
            qk_norm(2 * NH - 1)
            lo_part(pre_chunk(N_IN))
            lo_part(pre_chunk(N_IN + 1))

            def scores_max(a):
                s, w = 2 * (a % 2), P * (a % NT + 1)
                dve.wait_ge(sc_ready, a + 1)
                link(dve.tensor_tensor(acc[:, s:s + 2, w - P:w], acc[:, s:s + 2, w - P:w],
                                       causal[:].unsqueeze(1).broadcast_to([P, 2, P]), ALU.add))
                link(dve.tensor_reduce(small[:, NMAX + s:NMAX + s + 2], acc[:, s:s + 2, 0:w], AX_X, ALU.max))
                dve.tensor_scalar(small[:, NMAX + s:NMAX + s + 2], small[:, NMAX + s:NMAX + s + 2], -1.0, None,
                                  ALU.mult).then_inc(max_ready, 1)

            def weight_diff(a):
                s, w = 2 * (a % 2), P * (a % NT + 1)
                inv = small[:, SUMS + s:SUMS + s + 2]
                dve.wait_ge(exp_done, 2 * a + 2)
                link(dve.reciprocal(inv, inv))
                link(dve.tensor_tensor(inv[:, 1:2], inv[:, 1:2], small[:, LAM + 5:LAM + 6], ALU.mult))
                link(dve.tensor_scalar(wpart[:, 0:w], prob[a % 2][:, 0, 0:w], inv[:, 0:1], None, ALU.mult))
                if a >= 2:
                    dve.wait_ge(wt_ps, a - 1)
                dve.scalar_tensor_tensor(wdiff[a % 2][:, 0:w], prob[a % 2][:, 1, 0:w], inv[:, 1:2], wpart[:, 0:w],
                                         ALU.mult, ALU.add).then_inc(wd_ready, 1)

            def o_norm(a):
                dve.wait_ge(orstd_ready, a + 1)
                if a >= 2:
                    dve.wait_ge(ot_ps, a - 1)
                dve.tensor_scalar(o_n[a % 2][:], acc[:, 6, 0:P], small[:, ORS + a % 2:ORS + a % 2 + 1], None,
                                  ALU.mult).then_inc(on_ready, 1)

            for s in range(NA + 3):
                if s < NA:
                    scores_max(s)
                    weight_diff(s)
                if 2 <= s <= NA + 1:
                    o_norm(s - 2)
                if s >= 3 and (s - 3) % NT == NT - 1:
                    h = (s - 3) // NT
                    dve.wait_ge(ya_hi_ready, h + 1)
                    dve.scalar_tensor_tensor(ya_lo[:, h, :], acc[:, 7, :], vec[:, V_S8:V_S8 + 1],
                                             ya_hi[:, h, :].bitcast(F32), ALU.mult, ALU.subtract)\
                        .then_inc(ya_lo_ready, 1)

            def add_mix(j, t):
                wait_mix(dve, j, t)
                dst = xres[:, t, CC * j:CC * j + CC]
                dve.tensor_tensor(dst, acc[:, (j * NT + t) % 4, 0:CC], dst, ALU.add).then_inc(x1_done, 1)

            for j in range(N_OUT - 1):
                for t in range(NT):
                    add_mix(j, t)
                if j < 2:
                    lo_part(pre_chunk(N_IN + 2 + j))
            dve.wait_ge(gain_loaded, 32)

            def choose(t):
                dve.wait_ge(lg_ps, t + 1)
                link(dve.tensor_copy(lg[:], acc[:, 7, 0:E]))
                link(dve.max(top8[:], lg[:]))
                link(dve.max_index(idx8[:], top8[:], lg[:]))
                dve.tensor_scalar(g4[:, 6:7], top8[:, 0:1], -1.0, None, ALU.mult).then_inc(top_ready, 1)
                link(dve.tensor_copy(idxf[:], idx8[:]))
                for k in range(TOP_K):
                    link(dve.tensor_scalar(pick[:, k, :], iota_e[:], idxf[:, k:k + 1], None, ALU.is_equal))
                by_e = pick[:].rearrange("p k e -> p e k")
                link(dve.tensor_reduce(chosen[:, t, :], by_e, AX_X, ALU.add))
                link(dve.tensor_copy(chosen_bf[:, t, :], chosen[:, t, :]))
                link(dve.scalar_tensor_tensor(which[:, t, :], pick[:, 2, :], 2.0, pick[:, 1, :], ALU.mult, ALU.add))
                link(dve.scalar_tensor_tensor(which[:, t, :], pick[:, 3, :], 3.0, which[:, t, :], ALU.mult, ALU.add))
                dve.wait_ge(g4_ready, t + 1)
                link(dve.reciprocal(g4[:, 5:6], g4[:, 4:5]))
                link(dve.tensor_scalar(g4[:, 0:4], g4[:, 0:4], g4[:, 5:6], None, ALU.mult))
                for k in range(TOP_K):
                    link(dve.tensor_scalar(pickg[:, k, :], pick[:, k, :], g4[:, k:k + 1], None, ALU.mult))
                dve.tensor_reduce(gates[:, t, :], pickg[:].rearrange("p k e -> p e k"), AX_X, ALU.add)\
                    .then_inc(tile_routed, 1)

            for t in range(NT):
                add_mix(N_OUT - 1, t)
                dve.wait_ge(rstd2, t + 1)
                if t >= 2:
                    dve.wait_ge(h2_stored[t - 2], 16)
                    dve.wait_ge(h2t_ps, 2 * (t - 1))
                dve.scalar_tensor_tensor(h2[t % 2][:], xres[:, t, :], small[:, RS + t:RS + t + 1], gain[:],
                                         ALU.mult, ALU.mult).then_inc(h2_ready, 1)
                dve.wait_ge(h2t_ps, 2 * t + 2)
                if t >= 2:
                    dve.wait_ge(lgt_ps, t - 1)
                dve.tensor_copy(h2_t[t % 2][:, 4:8, :], acc[:, 5, :].rearrange("p (k n) -> p k n", k=4))\
                    .then_inc(h2t_vec, 1)
                if t >= 1:
                    choose(t - 1)
            choose(NT - 1)

            dve.wait_ge(rank_ps, 1)
            dve.wait_ge(consts_ready, 1)
            dve.wait_ge(route_zero, 1)
            by_e = "p (t e) -> p e t"
            chosen_e = chosen[:].rearrange("p t e -> p e t")
            link(dve.scalar_tensor_tensor(pos[:], acc[:, 6, 0:NT * E].rearrange(by_e, e=E), 1.0, chosen_e,
                                          ALU.add, ALU.mult))
            link(dve.tensor_scalar(pos[:], pos[:], -1.0, None, ALU.add))
            link(dve.tensor_copy(cnt[:, 0, :], acc[:, 6, NT * E:NT * E + E]))
            zeros = route[:, :, :, 3]
            link(dve.tensor_scalar(route[:, :, :, 1], zeros, part[:, 0:1], None, ALU.add))
            link(dve.tensor_scalar(route[:, :, :, 5], zeros, part[:, 0:1], float(TOP_K), ALU.add, ALU.mult))
            link(dve.tensor_copy(route[:, :, :, 6], which[:].rearrange("p t e -> p e t")))
            link(dve.tensor_copy(rest[:], gates[:].rearrange("p t e -> p e t")))
            for col in (8, 9, 10):
                link(dve.tensor_copy(route[:, :, :, col], rest[:]))
                if col < 10:
                    link(dve.tensor_tensor(rest[:], rest[:], route[:, :, :, col], ALU.subtract))
            more, total = cnt[:, 1, :], cnt[:, 2, :]
            link(dve.tensor_scalar(more, cnt[:, 0, :], float(SLOTS), None, ALU.is_gt))
            for m in range(2, T // SLOTS):
                link(dve.scalar_tensor_tensor(more, cnt[:, 0, :], float(SLOTS * m), more, ALU.is_gt, ALU.add))
            link(dve.memset(cnt[:, 3, :], 1.0))
            link(dve.tensor_tensor_scan(total, cnt[:, 3, :], more, 0.0, ALU.mult, ALU.add))
            wide = [P, EXTRA, E]
            link(dve.tensor_tensor(xtr[:, 0], total.unsqueeze(1).broadcast_to(wide), jot[:], ALU.is_le))
            link(dve.tensor_tensor(xtr[:, 1], xtr[:, 0], more.unsqueeze(1).broadcast_to(wide), ALU.mult))
            link(dve.tensor_reduce(xj[:, 0:2, :], xtr[:], AX_X, ALU.add))
            link(dve.tensor_scalar(item_e[:, E:ITEMS], xj[:, 0, :], float(E - 1), None, ALU.min))
            link(dve.tensor_copy(item_e[:, 0:E], iota_e[:]))
            link(dve.tensor_tensor(xj[:, 2, :], jot[:, :, 0], xj[:, 1, :], ALU.subtract))
            link(dve.tensor_scalar(xj[:, 2, :], xj[:, 2, :], 1.0, float(SLOTS), ALU.add, ALU.mult))
            link(dve.tensor_scalar(xj[:, 3, :], xj[:, 0, :], float(E), BIG, ALU.is_ge, ALU.mult))
            link(dve.tensor_tensor(item_off[:, E:ITEMS], xj[:, 2, :], xj[:, 3, :], ALU.add))
            link(dve.memset(item_off[:, 0:E], 0.0))
            dve.tensor_scalar(item_e[:, ITEMS:ITEMS + 1], total[:, E - 1:E], float(E), None, ALU.add)\
                .then_inc(tables_ready, 1)
            dve.wait_ge(tables_ready, 1)

            for t in range(NT):
                dve.wait_ge(h2_stored[t], 16)
            dve.wait_ge(lgt_ps, NT)
            link(dve.memset(xg[:], 0.0))
            dve.memset(b1row[:], 0.0).then_inc(rows_zero, 1)
            dve.memset(b2_sb[:], 0.0).then_inc(rows_zero, 1)
            for t in range(NT):
                link(dve.memset(g_t[t][:], 0.0))
            link(dve.memset(y_gate[:], 0.0))
            link(dve.memset(held[:], 0.0))

            def mark(n, e):
                for t in range(NT):
                    dve.tensor_scalar(onehot[:, t, :], iota_slot[:], item_off[:, bass.ds(n, 1)],
                                      pos[:, bass.ds(e, 1), t], ALU.add, ALU.is_equal)
                dve.tensor_copy(rcur[:], route[:, bass.ds(e, 1), :, :].rearrange("p o t c -> p (o t) c"))\
                    .then_inc(onehot_ready, 1)

            def learn(n):
                dve.wait_ge(learned_ps, n + 1)
                dve.tensor_reduce(learned[:], acc[:, 7, 0:12].rearrange("p (a b) -> p a b", b=4), AX_X, ALU.add)\
                    .then_inc(learned_ready, 1)
                dve.wait_ge(learned_ready, n + 1)
                dve.wait_ge(gathered, n * 16)
                dve.tensor_scalar(tok_idx[:], learned[:, 0:1], BIG, None, ALU.add).then_inc(idx_ready, 1)

            def shift(n):
                dve.tensor_copy(y_gate[:], held[:, 1:2]).then_inc(shift_own, 1)
                dve.tensor_scalar(y_idx[:], held[:, 0:1], BIG, None, ALU.add).then_inc(shift_own, 1)
                dve.wait_ge(shift_own, n * 2 + 2)
                dve.tensor_copy(held[:], learned[:, 1:3]).then_inc(shifted, 1)

            def xt_lo_half(g, hi_count):
                dve.wait_ge(xt_hi_ready, hi_count)
                dve.tensor_tensor(xt_lo[:, 4 * g:4 * g + 4, :], acc[:, 7, :].rearrange("p (k n) -> p k n", k=4),
                                  xt_hi[:, 4 * g:4 * g + 4, :].bitcast(F32), ALU.subtract).then_inc(xt_lo_ready, 1)

            mark(0, 0)
            learn(0)
            shift(0)
            for g in range(2):
                xt_lo_half(g, g + 1)
            n_items = load_n_items(dve)
            with dve.Fori(0, n_items) as i:
                for c in range(PER):
                    lo_part(item_chunk(i, c))
                    if c == 1:
                        e = dve.value_load(item_e[0:1, bass.ds(i + 1, 1)], min_val=0, max_val=E - 1)
                        mark(i + 1, e)
                    if c == 3:
                        learn(i + 1)
                    if c in (5, 9):
                        half = c // 4 - 1
                        dve.wait_ge(chunk_used, i * PER + PRE + 4 * half + 4)
                        dve.tensor_scalar(gate_c[:], acc[:, 2 * half, :], LIMIT, None, ALU.min).then_inc(gate_ready, 1)
                        dve.tensor_scalar(up_c[:], acc[:, 2 * half + 1, :], LIMIT, -LIMIT, ALU.min, ALU.max)\
                            .then_inc(up_ready, 1)
                        dve.wait_ge(up_ready, i * 4 + 2 * half + 1)
                        dve.wait_ge(gate_ready, i * 2 + half + 1)
                        dve.scalar_tensor_tensor(up_c[:], up_c[:], 1.0, gate_c[:], ALU.add, ALU.mult)\
                            .then_inc(up_ready, 1)
                        dve.wait_ge(up_ready, i * 4 + 2 * half + 2)
                        dve.wait_ge(sig_ready, i * 2 + half + 1)
                        dve.tensor_tensor(act[half][:], up_c[:], sig[:], ALU.mult).then_inc(act_ready, 1)
                    if c in (8, 11):
                        half = (c - 8) // 3
                        dve.wait_ge(at_hi_ready, i * 2 + half + 1)
                        dve.tensor_tensor(at_lo[half][:], acc[:, 6, :].rearrange("p (k n) -> p k n", k=4),
                                          at_hi[half][:].bitcast(F32), ALU.subtract).then_inc(at_lo_ready, 1)
                    if c == 10:
                        xt_lo_half(0, i * 2 + 3)
                xt_lo_half(1, i * 2 + 4)
                dve.wait_ge(y_stored, i * 16 + 16)
                shift(i + 1)

            for t in range(NT):
                dve.wait_ge(gt_ps, NT)
                dve.tensor_copy(g_t[t][0:E, :], acc[0:E, 6, P * t:P * t + P]).then_inc(gt_ready, 1)
            for t in range(NT):
                for h in range(2):
                    dve.wait_ge(b2_ps, 2 * t + h + 1)
                    dst = xres[:, t, 512 * h:512 * h + 512]
                    dve.tensor_tensor(dst, acc[:, 2 * (t % 2) + h, :], dst, ALU.add).then_inc(b2_added, 1)
            for t in range(NT):
                dve.wait_ge(b2_added, 2 * NT)
                for k in range(TOP_K):
                    s = 2 * (t % 3) + k // 2
                    if k % 2 == 0:
                        dve.wait_ge(y4_loaded[s], 16 * (t // 3 + 1))
                    ins = dve.tensor_tensor(xres[:, t, :], xres[:, t, :], columns(raw[s], 2)[:, k % 2, :], ALU.add)
                    if k < TOP_K - 1:
                        ins.then_inc(sum_own, 1)
                        dve.wait_ge(sum_own, 3 * t + k + 1)
                    else:
                        ins.then_inc(out_ready, 1)

        @block.tensor
        def _(pe):
            def wait_split(chunk):
                pe.wait_ge(lo_vec, chunk[0] + 1)
                pe.wait_ge(lo_pool, chunk[0] + 1)

            pe.wait_ge(ident_ready, 1)
            pe.wait_ge(vecs_loaded, 16 * 11)
            pe.transpose(acc[:, 7, 0:64], vec_rows, ident[0:64, 0:64]).then_inc(vec_t, 1)
            for t in range(NT):
                pe.wait_ge(xs_ready, t + 1)
                for g in range(2):
                    if t >= 2:
                        pe.wait_ge(ht_lo_ready, 2 * (t - 2) + g + 1)
                    for k in range(4):
                        ins = pe.transpose(acc[:, 2 * (t % 2) + g, P * k:P * k + P],
                                           xs[t % 2][:, P * (4 * g + k):P * (4 * g + k) + P], ident[:])
                    ins.then_inc(xt_ps, 1)

            def z_tile(u):
                chunk = pre_chunk(u // 2)
                col = P * (u % 2)
                if u % 2 == 0:
                    wait_split(chunk)
                if u == 0:
                    pe.wait_ge(ht_lo_ready, 2 * NT)
                if u >= 4:
                    wait_z_read(pe, u - 4)
                for k in range(KD):
                    w = [m[:, k, col:col + P] for m in parts(chunk)]
                    ins = three_passes(pe, acc[:, u % 4, :], w, (ht_hi[:, k, :], ht_lo[:, k, :]), k == 0, k == KD - 1)
                ins.then_inc(chunk_used if u % 2 else z_ready, 1)

            def v_piece(v):
                j, t = v // NT, v % NT
                chunk = pre_chunk(NU // 2 + j)
                if t == 0:
                    wait_split(chunk)
                wait_z_read(pe, NU + v - 4)
                for k in range(KD):
                    w = [m[:, k, :] for m in parts(chunk)]
                    h = [m[:, k, P * t:P * t + P] for m in (ht_hi, ht_lo)]
                    ins = three_passes(pe, acc[:, (NU + v) % 4, 0:CC], h, w, k == 0, k == KD - 1)
                ins.then_inc(chunk_used if t == NT - 1 else z_ready, 1)

            def lru_gate(c):
                pe.wait_ge(conv_done, c + 1)
                pe.wait_ge(bd_loaded, 64)
                if c >= 1:
                    pe.wait_ge(gate_read, c)
                pe.matmul(acc[:, 4, :], bd[:, c, :], xc[c % 2][:], start=True, stop=True)
                pe.matmul(acc[:, 5, :], bd[:, NC + c, :], xc[c % 2][:], start=True, stop=True).then_inc(gates_ready, 1)

            def head_squares(n):
                pe.wait_ge(qsq_ready, n + 1)
                pe.wait_ge(consts_ready, 1)
                if n >= 1:
                    pe.wait_ge(qrs_ready, n)
                pe.matmul(acc[:, 6, :], half_ones[:], (ga, gb)[n % 2][:], start=True, stop=True)\
                    .then_inc(qss_ready, 1)

            for u in range(NU):
                z_tile(u)
                if 1 <= u <= NC:
                    lru_gate(u - 1)
                if u >= U_Q + 1:
                    head_squares(u - U_Q - 1)
            for v in range(NV):
                v_piece(v)
                if v == 0:
                    head_squares(2 * NH - 1)

            def scores(a):
                h, b = a // NT, a % NT
                w = P * (b + 1)
                pe.wait_ge(qm_ready, 2 * h + 2)
                if a < 2:
                    pe.wait_ge(v_done, NV)
                else:
                    pe.wait_ge(exp_done, 2 * (a - 1))
                for c in range(2):
                    ins = pe.matmul(acc[:, 2 * (a % 2) + c, 0:w], qm[h % 2][:, c, P * b:P * b + P], k_sb[:, h, 0:w],
                                    start=True, stop=True)
                ins.then_inc(sc_ready, 1)

            def turn_weights(a):
                pe.wait_ge(wd_ready, a + 1)
                if a >= 2:
                    pe.wait_ge(wt_ready, a - 1)
                for k in range(a % NT + 1):
                    ins = pe.transpose(acc[:, 4 + a % 2, P * k:P * k + P], wdiff[a % 2][:, P * k:P * k + P], ident[:])
                ins.then_inc(wt_ps, 1)

            def times_v(a):
                h, b = a // NT, a % NT
                pe.wait_ge(wt_ready, a + 1)
                if a >= 1:
                    pe.wait_ge(on_ready, a)
                else:
                    pe.wait_ge(qrs_ready, 2 * NH)
                for k in range(b + 1):
                    ins = pe.matmul(acc[:, 6, 0:P], w_t[a % 2][:, P * k:P * k + P], v_sb[:, k, P * h:P * h + P],
                                    start=(k == 0), stop=(k == b))
                ins.then_inc(o_ready, 1)

            def turn_o(a):
                h, b = a // NT, a % NT
                pe.wait_ge(on_ready, a + 1)
                if b == 0 and h >= 1:
                    pe.wait_ge(ya_lo_ready, h)
                if a == 0:
                    pe.wait_ge(setup3, 1)
                pe.transpose(acc[:, 7, P * b:P * b + P], o_n[a % 2][:], ident[:]).then_inc(ot_ps, 1)

            for s in range(NA + 3):
                if s < NA:
                    scores(s)
                if 1 <= s <= NA:
                    turn_weights(s - 1)
                if 2 <= s <= NA + 1:
                    times_v(s - 2)
                if s >= 3:
                    turn_o(s - 3)

            for j in range(N_OUT):
                chunk = pre_chunk(N_IN + j)
                wait_split(chunk)
                if j == 0:
                    pe.wait_ge(yr_lo_ready, NC)
                    pe.wait_ge(ya_lo_ready, NH)
                    pe.wait_ge(exp_done, 2 * NA)
                for t in range(NT):
                    idx = j * NT + t
                    if idx >= 4:
                        pe.wait_ge(x1_done, idx - 3)
                    for k in range(KD):
                        w = [m[:, k, :] for m in parts(chunk)]
                        pair, c = ((yr_hi, yr_lo), k) if k < NC else ((ya_hi, ya_lo), k - NC)
                        y = [m[:, c, P * t:P * t + P] for m in pair]
                        ins = three_passes(pe, acc[:, idx % 4, 0:CC], y, w, k == 0, k == KD - 1)
                    ins.then_inc(chunk_used if t == NT - 1 else mix_ready, 1)
            pe.wait_ge(rw_loaded, 16)
            for t in range(NT):
                pe.wait_ge(h2_ready, t + 1)
                if t >= 1:
                    pe.wait_ge(h2t_act, t)
                    pe.wait_ge(h2t_vec, t)
                for g in range(2):
                    for k in range(4):
                        ins = pe.transpose(acc[:, 4 + g, P * k:P * k + P], h2[t % 2][:, P * (4 * g + k):P * (4 * g + k) + P],
                                           ident[:])
                    ins.then_inc(h2t_ps, 1)
                pe.wait_ge(h2t_act, t + 1)
                pe.wait_ge(h2t_vec, t + 1)
                if t >= 1:
                    pe.wait_ge(lgt_ready, t)
                for k in range(KD):
                    ins = pe.matmul(acc[0:E, 6, 0:P], rw[:, k, :], h2_t[t % 2][:, k, :], start=(k == 0), stop=(k == KD - 1))
                ins.then_inc(lgt_ps, 1)
                pe.wait_ge(lgt_ready, t + 1)
                if t >= 1:
                    pe.wait_ge(top_ready, t)
                pe.transpose(acc[:, 7, 0:E], lg_t[:], ident[0:E, 0:E]).then_inc(lg_ps, 1)

            pe.wait_ge(tile_routed, NT)
            for t in range(NT):
                for s in range(t):
                    pe.matmul(acc[:, 6, E * t:E * t + E], ones_bf[:], chosen_bf[:, s, :], start=(s == 0), stop=False)
                pe.matmul(acc[:, 6, E * t:E * t + E], before[:], chosen_bf[:, t, :], start=(t == 0), stop=True)
            for s in range(NT):
                ins = pe.matmul(acc[:, 6, E * NT:E * NT + E], ones_bf[:], chosen_bf[:, s, :], start=(s == 0), stop=(s == NT - 1))
            ins.then_inc(rank_ps, 1)

            def learn(n):
                pe.wait_ge(onehot_ready, n + 1)
                for t in range(NT):
                    ins = pe.matmul(acc[:, 7, 0:12], onehot[:, t, :], rcur[:, t, :], start=(t == 0), stop=(t == NT - 1))
                ins.then_inc(learned_ps, 1)

            def turn_xg(g):
                for k in range(4):
                    ins = pe.transpose(acc[:, 7, P * k:P * k + P], xg[:, P * (4 * g + k):P * (4 * g + k) + P], ident[:])
                ins.then_inc(xg_ps, 1)

            def turn_act(i, half):
                pe.wait_ge(act_ready, i * 2 + half + 1)
                for k in range(4):
                    ins = pe.transpose(acc[:, 6, P * k:P * k + P], act[half][:, P * k:P * k + P], ident[:])
                ins.then_inc(at_ps, 1)

            learn(0)
            pe.wait_ge(gathered, 16)
            pe.wait_ge(idx_ready, 1)
            turn_xg(0)
            pe.wait_ge(xt_lo_ready, 1)
            turn_xg(1)
            n_items = load_n_items(pe)
            with pe.Fori(0, n_items) as i:
                for c in range(PER):
                    chunk = item_chunk(i, c)
                    wait_split(chunk)
                    if c == 0:
                        pe.wait_ge(xt_lo_ready, i * 2 + 2)
                        pe.wait_ge(b1row_loaded, i * 16 + 16)
                    if c < 8:
                        half, rows, up = c // 4, c % 4 // 2, c % 2
                        if c % 4 == 0:
                            for g in range(2):
                                col = g * D + half * 512
                                ins = pe.matmul(acc[:, 2 * half + g, :], ones_bf[:], b1row[:, col:col + 512],
                                                start=True, stop=False)
                            if half:
                                ins.then_inc(b1row_used, 1)
                        for k in range(4):
                            w = [m[:, k, :] for m in parts(chunk, 4)]
                            xk = [m[:, 4 * rows + k, :] for m in (xt_hi, xt_lo)]
                            ins = three_passes(pe, acc[:, 2 * half + up, :], xk, w, False, rows == 1 and k == 3)
                    else:
                        half = (c - 8) // 2
                        if c % 2 == 0:
                            pe.wait_ge(at_lo_ready, i * 2 + half + 1)
                        if c == 8:
                            pe.wait_ge(y_copied, i + 1)
                        for k in range(2):
                            kk = 2 * (c % 2) + k
                            for n in range(2):
                                w = [m[:, k, 512 * n:512 * n + 512] for m in parts(chunk, 2)]
                                a = [m[half][:, kk, :] for m in (at_hi, at_lo)]
                                ins = three_passes(pe, acc[:, 4 + n, :], a, w, c == 8 and k == 0, c == 11 and k == 1)
                    ins.then_inc(chunk_used, 1)
                    if c == 2:
                        learn(i + 1)
                    if c == 6:
                        turn_act(i, 0)
                    if c == 8:
                        pe.wait_ge(gathered, i * 16 + 32)
                        turn_xg(0)
                    if c == 9:
                        turn_act(i, 1)
                        pe.wait_ge(xt_lo_ready, i * 2 + 3)
                        turn_xg(1)

            pe.wait_ge(at_lo_ready, n_items * 2)
            for t in range(NT):
                pe.transpose(acc[0:E, 6, P * t:P * t + P], gates[:, t, :], ident[:]).then_inc(gt_ps, 1)
            pe.wait_ge(b2_loaded, 16)
            pe.wait_ge(gt_ready, NT)
            for t in range(NT):
                for h in range(2):
                    if t >= 2:
                        pe.wait_ge(b2_added, 2 * (t - 2) + h + 1)
                    pe.matmul(acc[:, 2 * (t % 2) + h, :], g_t[t][:], b2_sb[:, 512 * h:512 * h + 512],
                              start=True, stop=True).then_inc(b2_ps, 1)


_INS = ["x", "norm1_g", "w_in", "conv_w", "conv_b", "lru_wa", "lru_ba", "lru_wx", "lru_bx", "lru_lambda",
        "q_norm_g", "k_norm_g", "lambda_q1", "lambda_k1", "lambda_q2", "lambda_k2", "subln_g", "w_out",
        "norm2_g", "router_w", "router_b", "w1", "b1", "w2", "b2"]


def kernel(**inputs):
    import numpy as np
    import concourse.bacc as bacc
    from concourse.bass_utils import run_bass_kernel_spmd

    nc = bacc.Bacc("TRN2", target_bir_lowering=False, num_devices=1)
    arrays, args = {}, []
    for name in _INS:
        a = np.ascontiguousarray(inputs[name])
        arrays[f"in_{name}"] = a
        args.append(nc.dram_tensor(f"in_{name}", a.shape, mybir.dt.from_np(a.dtype), kind="ExternalInput").ap())
    out = nc.dram_tensor("out", arrays["in_x"].shape, F32, kind="ExternalOutput").ap()
    layer_kernel(nc, *args, out)
    return run_bass_kernel_spmd(nc, [arrays], core_ids=[0]).results[0]["out"]
```

```python
import math
from contextlib import ExitStack

import concourse.bass as bass
from concourse import mybir

F32 = mybir.dt.float32
F32R = mybir.dt.float32r
BF16 = mybir.dt.bfloat16
U32 = mybir.dt.uint32
I32 = mybir.dt.int32
ALU = mybir.AluOpType
ACT = mybir.ActivationFunctionType
AX_X = mybir.AxisListType.X

P = 128
RAW = 6
RING = 12
HI = 4
CH = 2048
VEC_COLS = 1408
LRU_C = 8.0
TOP_K = 4
LIMIT = 7.0
ALPHA = 1.702
EPS = 1e-5
LAM_INIT = 0.8 - 0.6 * math.exp(0.0)
NEG = -1e30
BIG = float(1 << 20)
GELU_C = math.sqrt(2.0 / math.pi)
TINY = 1e-18
SLOTS = 128
BEGUN = 2


def layer_kernel(nc, x, norm1_g, w_in, conv_w, conv_b, lru_wa, lru_ba, lru_wx, lru_bx, lru_lambda,
                 q_norm_g, k_norm_g, lambda_q1, lambda_k1, lambda_q2, lambda_k2, subln_g, w_out,
                 norm2_g, router_w, router_b, w1, b1, w2, b2, out):
    T, D = x.shape[1], x.shape[2]
    NT = T // P
    KD = D // P
    DR = conv_b.shape[1]
    NC = DR // P
    NH = (w_in.shape[2] - 2 * DR) // 3 // P
    HD = q_norm_g.shape[1]
    E = w1.shape[1]
    CW = conv_w.shape[1]
    N_IN = w_in.shape[2] * KD // CH
    N_OUT = D * KD // CH
    CC = CH // KD
    PRE = N_IN + N_OUT
    PER = 12
    EXTRA = TOP_K * T // SLOTS
    ITEMS = E + EXTRA
    assert (T, D, DR, NH, HD, E, CC) == (512, 1024, 512, 4, 64, 32, 256) and PER == RING and RING % RAW == 0 and PER % HI == 0

    h2_rows = nc.dram_tensor("h2_rows", (T, D), F32, kind="Internal").ap()
    y_rows = nc.dram_tensor("y_rows", (TOP_K * T, D), F32, kind="Internal").ap()
    b1_parts = nc.dram_tensor("b1_parts", (3, E, 2 * D), BF16, kind="Internal").ap()

    ctx = ExitStack()
    with ctx:
        def sb(name, shape, dt=F32, stack=ctx):
            return stack.enter_context(nc.sbuf_tensor(name, shape, dt))

        def sem(name):
            return ctx.enter_context(nc.semaphore(name))

        acc = ctx.enter_context(nc.psum_tensor("acc", [P, 8, 512], F32))

        ident = sb("ident", [P, P])
        half_ones = sb("half_ones", [P, P])
        ident_bf = sb("ident_bf", [P, P], BF16)
        causal = sb("causal", [P, P], BF16)
        before = sb("before", [P, P], BF16)
        ones = sb("ones", [P, P])
        ones_bf = sb("ones_bf", [P, P], BF16)
        iota_slot = sb("iota_slot", [P, P], BF16)
        iota_e = sb("iota_e", [P, E])
        jot = sb("jot", [P, EXTRA, E], BF16)
        part = sb("part", [P, 1])
        consts = sb("consts", [P, 4])
        xres = sb("xres", [P, NT, D])
        vec = sb("vec", [P, 64])
        small = sb("small", [P, 64])
        route = sb("route", [P, E, NT, 12], BF16)
        pos = sb("pos", [P, E, NT])
        gates = sb("gates", [P, NT, E])
        item_e = sb("item_e", [P, ITEMS + 1], I32)
        item_off = sb("item_off", [P, ITEMS])
        raw_ctx = ExitStack()
        raw = [sb(f"raw{n}", [P, CH], stack=raw_ctx) for n in range(RAW)]
        raw_ctx.close()
        lo = [sb(f"lo{n}", [P, CH], F32R) for n in range(RAW)]
        hi = [sb(f"hi{n}", [P, CH], F32R) for n in range(HI)]

        V_CW, V_CB, V_BA, V_BX, V_LAM, V_QG, V_KG, V_SG, V_RB = 0, 16, 20, 24, 28, 32, 33, 34, 35
        V_HB, V_HBX, V_HL, V_NHL = 36, 40, 44, 48
        V_Q8, V_S8 = 52, 53

        C_EPS, C_ONE, C_TINY, C_HALF = 0, 1, 2, 3

        pre_ctx = ExitStack()
        qm = [sb("qm0", [P, NH, T], stack=pre_ctx), None]
        k_sb = sb("k_sb", [P, NH, T], stack=pre_ctx)
        v_sb = sb("v_sb", [P, NT, NH * P], stack=pre_ctx)
        lam4 = k_sb[:, 0, 0:4 * HD].rearrange("p (a d) -> p a d", a=4)
        b1_rows = qm[0][:, 0, :]
        b1_part = [qm[0][:, 1 + n, 0:256].bitcast(BF16) for n in range(3)]
        xs = [v_sb[:, 2 * n:2 * n + 2, :].rearrange("p t d -> p (t d)") for n in range(2)]
        yr_hi = sb("yr_hi", [P, NC, T], F32R, pre_ctx)
        yr_lo = sb("yr_lo", [P, NC, T], F32R, pre_ctx)
        gain = sb("gain", [P, D], stack=pre_ctx)
        rw = sb("rw", [P, KD, E], stack=pre_ctx)
        z_ctx = ExitStack()
        ht_hi = sb("ht_hi", [P, KD, T], F32R, z_ctx)
        ht_lo = sb("ht_lo", [P, KD, T], F32R, z_ctx)
        bd = sb("bd", [P, 2 * NC, P], stack=z_ctx)
        qrs = sb("qrs", [P, T], stack=z_ctx)
        rt = sb("rt", [P, T], stack=z_ctx)
        iw = sb("iw", [P, T], stack=z_ctx)
        decay = sb("decay", [P, T], stack=z_ctx)
        l1 = sb("l1", [P, T], stack=z_ctx)
        ga = sb("ga", [P, T], stack=z_ctx)
        gb = sb("gb", [P, T], stack=z_ctx)
        r_ctx = ExitStack()
        h_rnn = sb("h_rnn", [P, NC, T], stack=r_ctx)
        vec_rows = h_rnn[0:64, NC - 1, 0:P]
        r_ctx.close()
        qm[1] = sb("qm1", [P, NH, T], stack=z_ctx)
        z_ctx.close()
        a_ctx = ExitStack()
        ya_hi = sb("ya_hi", [P, NH, T], F32R, a_ctx)
        ya_lo = sb("ya_lo", [P, NH, T], F32R, a_ctx)
        s_ctx = ExitStack()
        prob = [sb(f"prob{n}", [P, 2, T], stack=s_ctx) for n in range(2)]
        wdiff = [sb(f"wdiff{n}", [P, T], stack=s_ctx) for n in range(2)]
        w_t = [sb(f"w_t{n}", [P, T], stack=s_ctx) for n in range(2)]
        o_c = sb("o_c", [P, T], stack=s_ctx)
        o_sq = sb("o_sq", [P, T], stack=s_ctx)
        o_rs = sb("o_rs", [P, T], stack=s_ctx)
        ya = sb("ya", [P, T], stack=s_ctx)
        s_ctx.close()
        h_ctx = ExitStack()
        sb("below", [P, 128], stack=h_ctx)
        lg_t = sb("lg_t", [E, P], stack=h_ctx)
        top8 = sb("top8", [P, 8], stack=h_ctx)
        idx8 = sb("idx8", [P, 8], U32, h_ctx)
        g4 = sb("g4", [P, 8], stack=h_ctx)
        pick = sb("pick", [P, TOP_K, E], stack=h_ctx)
        pickg = sb("pickg", [P, TOP_K, E], stack=h_ctx)
        chosen = sb("chosen", [P, NT, E], BF16, h_ctx)
        which = sb("which", [P, E], stack=h_ctx)
        rest = sb("rest", [P, E], stack=h_ctx)
        cnt = sb("cnt", [P, 5, E], stack=h_ctx)
        xtr = sb("xtr", [P, 2, EXTRA, E], stack=h_ctx)
        xj = sb("xj", [P, 4, EXTRA], stack=h_ctx)
        g_ctx = ExitStack()
        h2 = [sb(f"h2_{n}", [P, D], stack=g_ctx) for n in range(2)]
        h2sq = sb("h2sq", [P, D], stack=g_ctx)
        h2_t = [sb(f"h2_t{n}", [P, KD, P], stack=g_ctx) for n in range(2)]
        g_ctx.close()
        h_ctx.close()
        a_ctx.close()
        pre_ctx.close()

        m_ctx = ctx
        xg = sb("xg", [P, D], stack=m_ctx)
        xt_hi = sb("xt_hi", [P, KD, SLOTS], F32R, m_ctx)
        xt_lo = sb("xt_lo", [P, KD, SLOTS], F32R, m_ctx)
        b1row = sb("b1row", [P, 2 * D], BF16, m_ctx)
        gate_c = sb("gate_c", [P, 512], stack=m_ctx)
        up_c = sb("up_c", [P, 512], stack=m_ctx)
        sig = sb("sig", [P, 512], stack=m_ctx)
        act = [sb(f"act{n}", [P, 512], stack=m_ctx) for n in range(2)]
        at_hi = [sb(f"at_hi{n}", [P, 4, SLOTS], F32R, m_ctx) for n in range(2)]
        at_lo = [sb(f"at_lo{n}", [P, 4, SLOTS], F32R, m_ctx) for n in range(2)]
        y_sb = sb("y_sb", [P, D], stack=m_ctx)
        onehot = sb("onehot", [P, NT, SLOTS], BF16, m_ctx)
        rcur = sb("rcur", [P, NT, 12], BF16, m_ctx)
        learned = sb("learned", [P, 3], stack=m_ctx)
        tok_idx = sb("tok_idx", [P, 1], U32, m_ctx)
        held = sb("held", [P, 2], stack=m_ctx)
        y_idx = sb("y_idx", [P, 1], U32, m_ctx)
        y_gate = sb("y_gate", [P, 1], stack=m_ctx)
        b2_sb = sb("b2_sb", [P, D], stack=m_ctx)
        g_t = [sb(f"g_t{n}", [P, P], stack=m_ctx) for n in range(NT)]

        slot_ctx = ExitStack()
        raw += [sb(f"raw{n}", [P, CH], stack=slot_ctx) for n in (7, 8)]
        slot_ctx.close()
        lo += [sb(f"lo{n}", [P, CH], F32R, m_ctx) for n in (7, 8)]
        sb("between", [P, 1920], stack=m_ctx)
        raw += [sb(f"raw{n}", [P, CH], stack=slot_ctx) for n in (9, 10, 11, 6)]
        slot_ctx.close()
        lo += [sb(f"lo{n}", [P, CH], F32R, m_ctx) for n in (9, 10, 11, 6)]
        for slots in (raw, lo):
            slots.insert(RAW, slots.pop())

        chunk_used = sem("chunk_used")
        vec_zero = sem("vec_zero")
        qm_zero = sem("qm_zero")
        ws_ready = sem("ws_ready")
        osq_ready = sem("osq_ready")
        oss_ready = sem("oss_ready")
        ors_ready = sem("ors_ready")
        ya_ready = sem("ya_ready")
        z_ready = sem("z_ready")
        conv_done = sem("conv_done")
        yr_ready = sem("yr_ready")
        qk_done = sem("qk_done")
        v_done = sem("v_done")
        mix_ready = sem("mix_ready")
        tables_ready = sem("tables_ready")
        x_loaded = [sem(f"x_loaded{n}") for n in range(NT)]
        gain_loaded = sem("gain_loaded")
        lo_vec = sem("lo_vec")
        lo_pool = sem("lo_pool")
        raw_loaded = [sem(f"raw_loaded{n}") for n in range(RING)]
        y_stored = sem("y_stored")
        out_ready = sem("out_ready")
        y4_loaded = [sem(f"y4_loaded{n}") for n in range(2 * NT)]
        out_stored = sem("out_stored")
        pool_own = sem("pool_own")
        vecs_loaded = sem("vecs_loaded")
        ident_ready = sem("ident_ready")
        bd_loaded = sem("bd_loaded")
        lam_loaded = sem("lam_loaded")
        rw_loaded = sem("rw_loaded")
        b1_loaded = sem("b1_loaded")
        consts_ready = sem("consts_ready")
        hi_ready = sem("hi_ready")
        b1_stored = sem("b1_stored")
        route_zero = sem("route_zero")
        yr_hi_ready = sem("yr_hi_ready")
        yr_lo_ready = sem("yr_lo_ready")
        sc_ready = sem("sc_ready")
        gathered = sem("gathered")
        b1row_loaded = sem("b1row_loaded")
        h2_stored = [sem(f"h2_stored{n}") for n in range(NT)]
        idx_ready = sem("idx_ready")
        rows_zero = sem("rows_zero")
        b2_loaded = sem("b2_loaded")
        y_copied = sem("y_copied")
        xg_ps = sem("xg_ps")
        b1row_used = sem("b1row_used")
        last_y_copied = sem("last_y_copied")
        act_own = sem("act_own")
        xt_ps = sem("xt_ps")
        ht_hi_ready = sem("ht_hi_ready")
        rstd1 = sem("rstd1")
        setup1 = sem("setup1")
        setup2 = sem("setup2")
        xs_ready = sem("xs_ready")
        gates_ready = sem("gates_ready")
        setup3 = sem("setup3")
        h_done = sem("h_done")
        rt_ready = sem("rt_ready")
        gate_read = sem("gate_read")
        lns_ready = sem("lns_ready")
        lnd_ready = sem("lnd_ready")
        mul_ready = sem("mul_ready")
        gsq_ready = sem("gsq_ready")
        garg_ready = sem("garg_ready")
        gth_ready = sem("gth_ready")
        qss_ready = sem("qss_ready")
        qsq_ready = sem("qsq_ready")
        qrs_ready = sem("qrs_ready")
        ht_lo_ready = sem("ht_lo_ready")
        max_ready = sem("max_ready")
        wd_ready = sem("wd_ready")
        exp_done = sem("exp_done")
        wt_ps = sem("wt_ps")
        o_ready = sem("o_ready")
        wt_ready = sem("wt_ready")
        ya_hi_ready = sem("ya_hi_ready")
        top_ready = sem("top_ready")
        g4_ready = sem("g4_ready")
        x1_done = sem("x1_done")
        rstd2 = sem("rstd2")
        h2_ready = sem("h2_ready")
        h2t_ps = sem("h2t_ps")
        lgt_ps = sem("lgt_ps")
        h2t_act = sem("h2t_act")
        lg_ps = sem("lg_ps")
        lgt_ready = sem("lgt_ready")
        xt_hi_ready = sem("xt_hi_ready")
        shifted = sem("shifted")
        gate_ready = sem("gate_ready")
        sig_ready = sem("sig_ready")
        at_ps = sem("at_ps")
        at_hi_ready = sem("at_hi_ready")
        dve_own = sem("dve_own")
        vec_t = sem("vec_t")
        ya_lo_ready = sem("ya_lo_ready")
        tile_routed = sem("tile_routed")
        h2t_vec = sem("h2t_vec")
        rank_ps = sem("rank_ps")
        onehot_ready = sem("onehot_ready")
        learned_ps = sem("learned_ps")
        learned_ready = sem("learned_ready")
        shift_own = sem("shift_own")
        xt_lo_ready = sem("xt_lo_ready")
        up_ready = sem("up_ready")
        act_ready = sem("act_ready")
        at_lo_ready = sem("at_lo_ready")
        gt_ps = sem("gt_ps")
        gt_ready = sem("gt_ready")
        b2_ps = sem("b2_ps")
        b2_added = sem("b2_added")
        sum_own = sem("sum_own")

        def pre_chunk(n):
            return n, n % RAW, n % HI, 16 * (n // RAW + 1)

        def item_chunk(i, c):
            m, slot = PRE + c, (PRE + c) % RING
            before = len(range(slot, PRE, RAW)) if slot < RAW else 0
            return i * PER + m, slot, m % HI, i * 16 + 16 * (before + 1)

        def three_passes(pe, out_ap, weights, moving, first, last):
            pe.matmul(out_ap, weights[0], moving[0], start=first, stop=False)
            pe.matmul(out_ap, weights[0], moving[1], start=False, stop=False)
            return pe.matmul(out_ap, weights[1], moving[0], start=False, stop=last)

        def columns(t, k=KD):
            return t[:].rearrange("p (k n) -> p k n", k=k)

        def parts(chunk, k=KD):
            return columns(hi[chunk[2]], k), columns(lo[chunk[1]], k)

        FIRST = {"x": 0, "g": NC // 2, "q": NC, "k": NC + NH // 2, "v": NC + NH}
        NV = 2 * NT
        STEPS = [("x", n) for n in range(NC)] + [("v", n) for n in range(NT)] + [("k", n) for n in range(NH)] \
            + [("g", n) for n in range(NC)] + [("q", n) for n in range(NH)] + [("v", n) for n in range(NT, NV)]
        CHUNK, LAST, COLS = [], [], []
        for kind, n in STEPS:
            each = NT if kind == "v" else 2
            if n % each == 0:
                COLS.append(CC * (FIRST[kind] + n // each))
            CHUNK.append(len(COLS) - 1)
            LAST.append(n % each == each - 1)
        AT_Q, AT_G = STEPS.index(("q", 0)), STEPS.index(("g", 0))
        GATES = {1: 0, 3: 1, 6: 2, 8: 3}
        SPLIT = {0: 2, 2: 3, 4: 4, 6: 5, 8: 6, 10: 7, 12: 8, 14: 9, 16: 10, 18: 11, 20: 12}
        NA = NH * NT

        def head_of(s):
            kind, n = STEPS[s] if 0 <= s < len(STEPS) else ("", 0)
            return {"k": n, "q": NH + n}.get(kind)

        def wait_z(eng, s):
            if LAST[s]:
                eng.wait_ge(chunk_used, CHUNK[s] + 1)
            else:
                eng.wait_ge(z_ready, LAST[:s + 1].count(False))

        def wait_z_read(eng, s):
            kind, n = STEPS[s]
            if kind == "x":
                eng.wait_ge(conv_done, n + 1)
            elif kind == "v":
                eng.wait_ge(v_done, n + 1)
            elif kind == "g":
                eng.wait_ge(yr_ready, n + 1)
            else:
                eng.wait_ge(qk_done, head_of(s) + 1)

        def wait_mix(eng, t, g):
            if t == NT - 1:
                eng.wait_ge(chunk_used, N_IN + 2 * g + 2)
            else:
                eng.wait_ge(mix_ready, 2 * t + g + 1)

        def load_n_items(eng):
            eng.wait_ge(tables_ready, 1)
            return eng.value_load(item_e[0:1, ITEMS:ITEMS + 1], min_val=E, max_val=ITEMS - 1)

        SS, RS, TMP, SOFT, LAM = 0, 4, 8, 12, 56
        SUMS, NMAX, INV = 36, 40, 44

        block = ctx.enter_context(nc.Block())

        @block.sync
        def _(sp):
            for t in range(NT):
                sp.dma_start(xres[:, t, :], x[0, P * t:P * t + P, :]).then_inc(x_loaded[t], 16)
                if t == 0:
                    sp.dma_start(gain[:], norm1_g.broadcast_to([P, D])).then_inc(gain_loaded, 16)

            sp.wait_ge(vec_zero, 1)
            sp.dma_start(vec_rows[V_CW:V_CW + 16, :], conv_w[0].rearrange("j (c p) -> (j c) p", p=P))\
                .then_inc(vecs_loaded, 16)
            for at, v in ((V_CB, conv_b), (V_BA, lru_ba), (V_BX, lru_bx), (V_LAM, lru_lambda)):
                sp.dma_start(vec_rows[at:at + NC, :], v[0].rearrange("(c p) -> c p", p=P)).then_inc(vecs_loaded, 16)
            for at, v in ((V_QG, q_norm_g), (V_KG, k_norm_g)):
                sp.dma_start(vec_rows[at:at + 1, :].rearrange("o (h d) -> o h d", h=2),
                             v.unsqueeze(1).broadcast_to([1, 2, HD])).then_inc(vecs_loaded, 16)
            sp.dma_start(vec_rows[V_SG:V_SG + 1, :], subln_g).then_inc(vecs_loaded, 16)
            sp.dma_start(vec_rows[V_RB:V_RB + 1, 0:E], router_b).then_inc(vecs_loaded, 16)

            for n in range(PRE):
                if n >= RAW:
                    sp.wait_ge(chunk_used, n - RAW + 1)
                w, col = (w_in, COLS[n]) if n < N_IN else (w_out, CC * (n - N_IN))
                sp.dma_start(columns(raw[n % RAW]), w[0].rearrange("(k p) n -> p k n", p=P)[:, :, col:col + CC])\
                    .then_inc(raw_loaded[n % RAW], 16)
                if n == 0:
                    for k, v in enumerate((lambda_q1, lambda_k1, lambda_q2, lambda_k2)):
                        sp.dma_start(lam4[:, k, :], v.broadcast_to([P, HD])).then_inc(lam_loaded, 16)

            def load_item(i, e, first=False):
                w1e = w1[0, bass.ds(e, 1)].rearrange("o (k p) n -> p (o k) n", p=P)
                w2e = w2[0, bass.ds(e, 1)].rearrange("o (k p) n -> p (o k) n", p=P)
                for c in range(PER):
                    n, slot, _, _ = item_chunk(i, c)
                    if not first:
                        sp.wait_ge(chunk_used, n - RING + 1)
                    elif slot < RAW:
                        if c >= RING - 2:
                            sp.wait_ge(gathered, 16)
                        sp.wait_ge(chunk_used, len(range(slot, PRE, RAW)) * RAW - RAW + slot + 1)
                    elif slot == 6:
                        sp.wait_ge(sc_ready, NA)
                    elif slot < 9:
                        sp.wait_ge(chunk_used, PRE)
                    else:
                        for t in range(NT):
                            sp.wait_ge(h2_stored[t], 16)
                        sp.wait_ge(lgt_ps, NT)
                        if slot > 9:
                            sp.wait_ge(gathered, 16)
                    if c < 8:
                        half, rows, up = c // 4, c % 4 // 2, c % 2
                        col = up * D + half * 512
                        src = w1e[:, 4 * rows:4 * rows + 4, col:col + 512]
                        dst = columns(raw[slot], 4)
                    else:
                        src = w2e[:, 2 * (c - 8):2 * (c - 8) + 2, :]
                        dst = columns(raw[slot], 2)
                    sp.dma_start(dst, src).then_inc(raw_loaded[slot], 16)

            load_item(0, 0, first=True)
            with sp.Fori(1, E) as i:
                load_item(i, i)
            n_items = load_n_items(sp)
            with sp.If(n_items > E):
                with sp.Fori(E, n_items) as i:
                    e = sp.value_load(item_e[0:1, bass.ds(i, 1)], min_val=0, max_val=E - 1)
                    load_item(i, e)

            sp.wait_ge(chunk_used, n_items * PER + PRE)
            sp.wait_ge(y_stored, 16 * (n_items + 1))
            for t in range(NT):
                for h in range(2):
                    sp.dma_start(columns(raw[2 * t + h], 2), y_rows[TOP_K * P * t:TOP_K * P * (t + 1), :]
                                 .rearrange("(p k) d -> p k d", k=TOP_K)[:, 2 * h:2 * h + 2, :])\
                        .then_inc(y4_loaded[2 * t + h], 16)
            for t in range(NT):
                sp.wait_ge(out_ready, t + 1)
                sp.dma_start(out[0, P * t:P * (t + 1), :], xres[:, t, :]).then_inc(out_stored, 16)
            sp.wait_ge(out_stored, 16 * NT)

        @block.gpsimd
        def _(pool):
            own = [0]

            def link(ins):
                own[0] += 1
                ins.then_inc(pool_own, 1)
                pool.wait_ge(pool_own, own[0])

            pool.memset(vec_rows, 0.0).then_inc(vec_zero, 1)
            for col, value in ((C_EPS, EPS), (C_ONE, 1.0), (C_TINY, TINY), (C_HALF, -0.5 * math.log(2.0))):
                link(pool.memset(consts[:, col:col + 1], value))
            link(pool.memset(ident[:], 0.0))
            pool.affine_select(out=ident[:], in_=ident[:], compare_op=ALU.not_equal, fill=1.0, base=0,
                               pattern=[[-1, P]], channel_multiplier=1).then_inc(ident_ready, 1)
            link(pool.memset(bd[:], 0.0))
            for g, w in ((0, lru_wa), (1, lru_wx)):
                for h in range(2):
                    pool.dma_start(bd[HD * h:HD * h + HD, NC * g:NC * g + NC, HD * h:HD * h + HD],
                                   w[0].rearrange("(c h) i j -> h i c j", h=2)[h]).then_inc(bd_loaded, 16)
            pool.dma_start(rw[:], router_w[0].rearrange("(k p) e -> p k e", p=P)).then_inc(rw_loaded, 16)
            pool.dma_start(b1_rows, b1[0].rearrange("e (q n) -> (e q) n", n=512)).then_inc(b1_loaded, 16)
            link(pool.memset(ones[:], 1.0))
            link(pool.memset(half_ones[:], 0.0))
            link(pool.memset(half_ones[0:64, 0:64], 1.0))
            link(pool.memset(half_ones[64:P, 64:P], 1.0))
            link(pool.memset(causal[:], 0.0))
            link(pool.affine_select(out=causal[:], in_=causal[:], compare_op=ALU.is_ge, fill=NEG, base=0,
                                    pattern=[[-1, P]], channel_multiplier=1))
            pool.wait_ge(ident_ready, 1)
            link(pool.tensor_copy(ident_bf[:], ident[:]))
            link(pool.memset(ones_bf[:], 1.0))
            link(pool.affine_select(out=before[:], in_=ones_bf[:], compare_op=ALU.is_gt, fill=0.0, base=0,
                                    pattern=[[1, P]], channel_multiplier=-1))
            link(pool.iota(iota_slot[:], pattern=[[1, P]], base=0, channel_multiplier=0,
                           allow_small_or_imprecise_dtypes=True))
            link(pool.iota(iota_e[:], pattern=[[1, E]], base=0, channel_multiplier=0,
                           allow_small_or_imprecise_dtypes=True))
            link(pool.iota(jot[:], pattern=[[1, EXTRA], [0, E]], base=0, channel_multiplier=0,
                           allow_small_or_imprecise_dtypes=True))
            pool.iota(part[:], pattern=[[0, 1]], base=0, channel_multiplier=1,
                      allow_small_or_imprecise_dtypes=True).then_inc(consts_ready, 1)

            def lo_part(chunk):
                n, slot, s, _ = chunk
                pool.wait_ge(hi_ready, n + 1)
                pool.tensor_tensor(lo[slot][:, VEC_COLS:CH], raw[slot][:, VEC_COLS:CH],
                                   hi[s][:, VEC_COLS:CH].bitcast(F32), ALU.subtract).then_inc(lo_pool, 1)

            for n in range(3):
                lo_part(pre_chunk(n))
            pool.wait_ge(b1_loaded, 16)
            for j in range(3):
                link(pool.tensor_copy(b1_part[j], b1_rows))
                pool.dma_start(b1_parts[j].rearrange("e (q n) -> (e q) n", n=512), b1_part[j]).then_inc(b1_stored, 16)
                if j < 2:
                    link(pool.tensor_tensor(b1_rows, b1_rows, b1_part[j], ALU.subtract))
                lo_part(pre_chunk(3 + j))
            link(pool.memset(route[:], 0.0))
            for t in range(NT):
                link(pool.memset(route[:, :, t, 0:1], float(P * t)))
                link(pool.memset(route[:, :, t, 4:5], float(TOP_K * P * t)))
            link(pool.memset(route[:, :, :, 2:3], -BIG))
            link(pool.memset(route[:, :, :, 7:8], -BIG))
            link(pool.iota(route[:, :, :, 1], pattern=[[0, E], [0, NT]], base=0, channel_multiplier=1,
                           allow_small_or_imprecise_dtypes=True))
            link(pool.iota(route[:, :, :, 5], pattern=[[0, E], [0, NT]], base=0, channel_multiplier=TOP_K,
                           allow_small_or_imprecise_dtypes=True))
            pool.memset(item_off[:, 0:E], 0.0).then_inc(route_zero, 1)
            for n in range(6, N_IN):
                lo_part(pre_chunk(n))
            pool.wait_ge(b1_stored, 48)
            pool.memset(qm[0][:], 0.0).then_inc(qm_zero, 1)
            pool.wait_ge(yr_ready, NC)
            pool.memset(qm[1][:], 0.0).then_inc(qm_zero, 1)
            for n in range(N_IN, PRE):
                lo_part(pre_chunk(n))
            def load_b1(n, e):
                pool.dma_start(b1row[0:3, :], b1_parts[:, bass.ds(e, 1), :].rearrange("j o n -> j (o n)"))\
                    .then_inc(b1row_loaded, 16)

            pool.wait_ge(o_ready, NA)
            pool.memset(xg[:], 0.0).then_inc(rows_zero, 1)
            pool.memset(b1row[:], 0.0).then_inc(rows_zero, 1)
            pool.wait_ge(rows_zero, 2)
            load_b1(0, 0)
            pool.wait_ge(h2_ready, NT)
            pool.wait_ge(lgt_ps, NT)
            pool.memset(b2_sb[:], 0.0).then_inc(rows_zero, 1)
            for t in range(NT):
                pool.memset(g_t[t][:], 0.0).then_inc(rows_zero, 1)
            pool.memset(y_gate[:], 0.0).then_inc(rows_zero, 1)
            pool.memset(held[:], 0.0).then_inc(rows_zero, 1)

            def gather():
                pool.indirect_dma_start(xg[:], None, h2_rows, bass.IndirectOffsetOnAxis(ap=tok_idx[:, 0:1], axis=0),
                                        bounds_check=T - 1, oob_is_err=False).then_inc(gathered, 16)

            def scatter():
                pool.indirect_dma_start(y_rows, bass.IndirectOffsetOnAxis(ap=y_idx[:, 0:1], axis=0), y_sb[:], None,
                                        bounds_check=TOP_K * T - 1, oob_is_err=False).then_inc(y_stored, 16)

            for t in range(NT):
                pool.wait_ge(h2_stored[t], 16)
            pool.wait_ge(rows_zero, 3)
            pool.wait_ge(idx_ready, 1)
            gather()
            pool.dma_start(b2_sb[0:E, :], b2[0]).then_inc(b2_loaded, 16)
            for c in range(BEGUN):
                lo_part(item_chunk(0, c))

            def item(i, begun=0):
                for c in range(PER):
                    if c == 2:
                        pool.wait_ge(y_copied, i + 1)
                    if c == 4:
                        pool.wait_ge(xg_ps, i * 2 + 2)
                        pool.wait_ge(idx_ready, i + 2)
                    if c == 5:
                        pool.wait_ge(b1row_used, i + 1)
                    if c >= begun:
                        lo_part(item_chunk(i, c))
                    if c == 2:
                        scatter()
                    if c == 4:
                        gather()
                    if c == 5:
                        load_b1(i + 1, pool.value_load(item_e[0:1, bass.ds(i + 1, 1)], min_val=0, max_val=E - 1))

            n_items = load_n_items(pool)
            item(0, BEGUN)
            with pool.Fori(1, n_items) as i:
                item(i)
            pool.wait_ge(last_y_copied, 1)
            scatter()

        @block.scalar
        def _(sc):
            own = [0]

            def link(ins):
                own[0] += 1
                ins.then_inc(act_own, 1)
                sc.wait_ge(act_own, own[0])

            def hi_part(chunk):
                n, slot, s, loads = chunk
                sc.wait_ge(raw_loaded[slot], loads)
                if not isinstance(n, int) or n >= HI:
                    sc.wait_ge(chunk_used, n - HI + 1)
                sc.activation(hi[s][:], raw[slot][:], ACT.Copy).then_inc(hi_ready, 1)

            def rstd(out_ap, in_ap, scale, tmp):
                link(sc.activation(tmp, in_ap, ACT.Ln, bias=consts[:, C_EPS:C_EPS + 1], scale=scale))
                return sc.activation(out_ap, tmp, ACT.Exp, scale=-0.5)

            LOG_EXP, SIGMOID = "natural_log_exp_and_others", "sigmoid_and_others"
            sc.preload_act_table_set(LOG_EXP)

            scratch = h_rnn[:].rearrange("p c t -> p (c t)")[:, 0:D]

            def ht_hi_tile(t):
                for g in range(2):
                    sc.wait_ge(xt_ps, 2 * t + g + 1)
                    sc.activation(ht_hi[:, 4 * g:4 * g + 4, P * t:P * t + P],
                                  acc[:, (2 * t + g) % 7, :].rearrange("p (k n) -> p k n", k=4),
                                  ACT.Copy).then_inc(ht_hi_ready, 1)

            sc.wait_ge(ident_ready, 1)
            for t in range(NT):
                sc.wait_ge(x_loaded[t], 16)
                link(sc.activation(scratch, xres[:, t, :], ACT.Square, accum_out=small[:, SS + t:SS + t + 1]))
                rstd(small[:, RS + t:RS + t + 1], small[:, SS + t:SS + t + 1], 1.0 / D,
                     small[:, TMP:TMP + 1]).then_inc(rstd1, 1)
                if t >= 1:
                    ht_hi_tile(t - 1)
            hi_part(pre_chunk(0))
            ht_hi_tile(NT - 1)
            hi_part(pre_chunk(1))
            sc.wait_ge(setup1, 1)
            link(sc.activation(small[:, SOFT + 4:SOFT + 8], small[:, SOFT:SOFT + 4], ACT.Exp, scale=-1.0))
            sc.activation(small[:, LAM + 2:LAM + 4], small[:, LAM:LAM + 2], ACT.Exp).then_inc(setup2, 1)
            sc.wait_ge(xs_ready, NT)
            sc.dma_start(gain[:], norm2_g.broadcast_to([P, D])).then_inc(gain_loaded, 16)

            def lru_gates(c):
                sc.wait_ge(gates_ready, c + 1)
                sc.wait_ge(setup3, 1)
                if c >= 1:
                    sc.wait_ge(h_done, c)
                sc.activation(rt[:], acc[:, 4, :], ACT.Tanh, bias=vec[:, V_HB + c:V_HB + c + 1], scale=0.5)\
                    .then_inc(rt_ready, 1)
                sc.activation(iw[:], acc[:, 5, :], ACT.Tanh, bias=vec[:, V_HBX + c:V_HBX + c + 1], scale=0.5)\
                    .then_inc(gate_read, 1)
                sc.wait_ge(rt_ready, c + 1)
                link(sc.activation(decay[:], rt[:], ACT.Exp, bias=vec[:, V_NHL + c:V_NHL + c + 1],
                                   scale=vec[:, V_NHL + c:V_NHL + c + 1]))
                link(sc.activation(rt[:], rt[:], ACT.Tanh, bias=vec[:, V_HL + c:V_HL + c + 1],
                                   scale=vec[:, V_HL + c:V_HL + c + 1]))
                sc.preload_act_table_set(LOG_EXP)
                link(sc.activation(l1[:], rt[:], ACT.Ln, bias=consts[:, C_ONE:C_ONE + 1]))
                sc.activation(rt[:], rt[:], ACT.Ln, bias=consts[:, C_TINY:C_TINY + 1]).then_inc(lns_ready, 1)
                sc.wait_ge(lnd_ready, c + 1)
                sc.activation(l1[:], rt[:], ACT.Exp, bias=consts[:, C_HALF:C_HALF + 1], scale=0.5)\
                    .then_inc(mul_ready, 1)

            def gelu(c):
                u = AT_G + c
                wait_z(sc, u)
                if c == 0:
                    sc.wait_ge(qss_ready, NH)
                sc.activation(ga[:], acc[:, u % 4, :], ACT.Square).then_inc(gsq_ready, 1)
                sc.wait_ge(garg_ready, c + 1)
                sc.activation(gb[:], ga[:], ACT.Tanh, scale=GELU_C).then_inc(gth_ready, 1)
                sc.wait_ge(yr_ready, c + 1)
                sc.activation(yr_hi[:, c, :], gb[:], ACT.Copy).then_inc(yr_hi_ready, 1)

            squares = [ga, gb, rt, l1]

            def qk_square(s):
                n = head_of(s)
                wait_z(sc, s)
                if n in (NH, NH + 1):
                    sc.wait_ge(h_done, NC)
                elif n >= 2:
                    sc.wait_ge(qss_ready, n - 1)
                sc.activation(squares[n // NH * 2 + n % 2][:], acc[:, s % 4, :], ACT.Square).then_inc(qsq_ready, 1)

            def qk_rstd(n):
                sc.wait_ge(qss_ready, n + 1)
                if n >= 1:
                    sc.wait_ge(qk_done, n)
                rstd(qrs[:], acc[:, 6, :], 1.0 / HD, qrs[:]).then_inc(qrs_ready, 1)

            def v_copy(s, v):
                wait_z(sc, s)
                if v == 0:
                    sc.wait_ge(ht_lo_ready, 2 * NT)
                j, t = v // NT, v % NT
                sc.activation(v_sb[:, t, CC * j:CC * j + CC], acc[:, s % 4, 0:CC], ACT.Copy).then_inc(v_done, 1)

            for s, (kind, n) in enumerate(STEPS):
                if s == AT_Q:
                    sc.preload_act_table_set(LOG_EXP)
                if s in SPLIT:
                    hi_part(pre_chunk(SPLIT[s]))
                if kind == "v":
                    v_copy(s, n)
                if kind == "g":
                    gelu(n)
                if head_of(s) is not None:
                    qk_square(s)
                if head_of(s - 1) is not None:
                    qk_rstd(head_of(s - 1))
                if s in GATES:
                    lru_gates(GATES[s])

            def scores_exp(a):
                w = P * (a // NH + 1)
                sc.wait_ge(max_ready, a + 1)
                if a == 0:
                    sc.wait_ge(chunk_used, N_IN)
                if a >= 2:
                    sc.wait_ge(wd_ready, a - 1)
                for c in range(2):
                    k = 2 * (a % 2) + c
                    sc.activation(prob[a % 2][:, c, 0:w], acc[:, k, 0:w], ACT.Exp, bias=small[:, NMAX + k:NMAX + k + 1],
                                  accum_out=small[:, SUMS + k:SUMS + k + 1]).then_inc(exp_done, 1)

            def scale_weights(a):
                w, k = P * (a // NH + 1), INV + 2 * (a % 2)
                sc.wait_ge(wd_ready, a + 1)
                sc.activation(wdiff[a % 2][:, 0:w], wdiff[a % 2][:, 0:w], ACT.Copy, scale=small[:, k:k + 1])\
                    .then_inc(ws_ready, 1)

            def weights_out(a):
                w = P * (a // NH + 1)
                sc.wait_ge(wt_ps, a + 1)
                if a >= 2:
                    sc.wait_ge(o_ready, a - 1)
                sc.activation(w_t[a % 2][:, 0:w], acc[:, 4 + a % 2, 0:w], ACT.Copy).then_inc(wt_ready, 1)

            def o_squares(b):
                sc.wait_ge(o_ready, NH * (b + 1))
                if b >= 1:
                    sc.wait_ge(ya_ready, b)
                sc.activation(o_c[:], acc[:, 6 + b % 2, :], ACT.Copy).then_inc(osq_ready, 1)
                sc.activation(o_sq[:], acc[:, 6 + b % 2, :], ACT.Square).then_inc(osq_ready, 1)

            def o_rstd(b):
                sc.wait_ge(oss_ready, b + 1)
                rstd(o_rs[:], acc[:, 6 + b % 2, :], 1.0 / P, o_rs[:]).then_inc(ors_ready, 1)

            for s in range(NA + 7):
                if s == 1:
                    hi_part(pre_chunk(PRE - 1))
                if s < NA:
                    scores_exp(s)
                if 1 <= s <= NA:
                    scale_weights(s - 1)
                if 2 <= s <= NA + 1:
                    weights_out(s - 2)
                if 6 <= s <= NA + 2 and s % NH == 2:
                    o_squares((s - 6) // NH)
                if s >= 8 and s % NH == 0:
                    o_rstd((s - 8) // NH)
                if s >= 9 and s % NH == 1:
                    b = (s - 9) // NH
                    sc.wait_ge(ya_ready, b + 1)
                    sc.activation(ya_hi[:, :, P * b:P * b + P], ya[:].rearrange("p (h n) -> p h n", h=NH), ACT.Copy)\
                        .then_inc(ya_hi_ready, 1)

            def gate_exp(t):
                sc.wait_ge(top_ready, t + 1)
                sc.activation(g4[:, 0:4], top8[:, 0:4], ACT.Exp, bias=g4[:, 6:7], accum_out=g4[:, 4:5])\
                    .then_inc(g4_ready, 1)

            def logits_out(t):
                sc.wait_ge(lgt_ps, t + 1)
                if t >= 1:
                    sc.wait_ge(lg_ps, t)
                sc.activation(lg_t[:], acc[0:E, 6, 0:P], ACT.Identity, bias=vec[0:E, V_RB:V_RB + 1])\
                    .then_inc(lgt_ready, 1)

            for t in range(NT):
                sc.wait_ge(x1_done, 2 * t + 2)
                link(sc.activation(h2sq[:], xres[:, t, :], ACT.Square, accum_out=small[:, SS + t:SS + t + 1]))
                rstd(small[:, RS + t:RS + t + 1], small[:, SS + t:SS + t + 1], 1.0 / D,
                     small[:, TMP:TMP + 1]).then_inc(rstd2, 1)
                if t >= 1:
                    logits_out(t - 1)
                sc.wait_ge(h2_ready, t + 1)
                sc.dma_start(h2_rows[P * t:P * t + P, :], h2[t % 2][:]).then_inc(h2_stored[t], 16)
                sc.wait_ge(h2t_ps, 2 * t + 1)
                if t >= 2:
                    sc.wait_ge(lgt_ps, t - 1)
                sc.activation(h2_t[t % 2][:, 0:4, :], acc[:, 4, :].rearrange("p (k n) -> p k n", k=4),
                              ACT.Copy).then_inc(h2t_act, 1)
                if t >= 1:
                    gate_exp(t - 1)
            logits_out(NT - 1)
            gate_exp(NT - 1)

            sc.preload_act_table_set(SIGMOID)

            def xt_hi_half(g, count):
                sc.wait_ge(xg_ps, count)
                sc.activation(xt_hi[:, 4 * g:4 * g + 4, :], acc[:, 7, :].rearrange("p (k n) -> p k n", k=4),
                              ACT.Copy).then_inc(xt_hi_ready, 1)

            def copy_y(n, done):
                sc.wait_ge(chunk_used, n * PER + PRE)
                sc.wait_ge(shifted, n + 1)
                sc.activation(y_sb[:].rearrange("p (h n) -> p h n", h=2), acc[:, 4:6, :], ACT.Copy,
                              scale=y_gate[:, 0:1]).then_inc(done, 1)

            def item(i, begun=0):
                for c in range(PER):
                    if c >= begun:
                        hi_part(item_chunk(i, c))
                    if c == 1:
                        copy_y(i, y_copied)
                    if c in (7, 10):
                        half = (c - 7) // 3
                        sc.wait_ge(gate_ready, i * 2 + half + 1)
                        sc.activation(sig[:], gate_c[:], ACT.Sigmoid, scale=ALPHA).then_inc(sig_ready, 1)
                    if c in (8, 11):
                        half = (c - 8) // 3
                        sc.wait_ge(at_ps, i * 2 + half + 1)
                        sc.activation(at_hi[half][:], acc[:, 6, :].rearrange("p (k n) -> p k n", k=4),
                                      ACT.Copy).then_inc(at_hi_ready, 1)
                    if c == 10:
                        xt_hi_half(0, i * 2 + 3)
                xt_hi_half(1, i * 2 + 4)

            for c in range(BEGUN):
                hi_part(item_chunk(0, c))
            for g in range(2):
                xt_hi_half(g, g + 1)
            n_items = load_n_items(sc)
            item(0, BEGUN)
            with sc.Fori(1, n_items) as i:
                item(i)
            copy_y(n_items, last_y_copied)

        @block.vector
        def _(dve):
            own = [0]

            def link(ins):
                own[0] += 1
                ins.then_inc(dve_own, 1)
                dve.wait_ge(dve_own, own[0])

            def lo_part(chunk):
                n, slot, s, _ = chunk
                dve.wait_ge(hi_ready, n + 1)
                dve.tensor_tensor(lo[slot][:, 0:VEC_COLS], raw[slot][:, 0:VEC_COLS],
                                  hi[s][:, 0:VEC_COLS].bitcast(F32), ALU.subtract).then_inc(lo_vec, 1)

            def ht_lo_tile(t):
                for g in range(2):
                    dst = (slice(None), slice(4 * g, 4 * g + 4), slice(P * t, P * t + P))
                    dve.wait_ge(ht_hi_ready, 2 * t + g + 1)
                    dve.tensor_tensor(ht_lo[dst], acc[:, (2 * t + g) % 7, :].rearrange("p (k n) -> p k n", k=4),
                                      ht_hi[dst].bitcast(F32), ALU.subtract).then_inc(ht_lo_ready, 1)

            dve.wait_ge(gain_loaded, 16)
            for t in range(NT):
                dve.wait_ge(rstd1, t + 1)
                if t >= 2:
                    dve.wait_ge(xt_ps, 2 * (t - 1))
                dve.scalar_tensor_tensor(xs[t % 2], xres[:, t, :], small[:, RS + t:RS + t + 1], gain[:],
                                         ALU.mult, ALU.mult).then_inc(xs_ready, 1)
                if t >= 1:
                    ht_lo_tile(t - 1)
            lo_part(pre_chunk(0))
            ht_lo_tile(NT - 1)
            lo_part(pre_chunk(1))

            dve.wait_ge(vec_t, 1)
            link(dve.tensor_copy(vec[:], acc[:, 7, 0:64]))
            soft = small[:, SOFT:SOFT + 4]
            nlam = small[:, SOFT + 8:SOFT + 12]
            link(dve.tensor_scalar(nlam, vec[:, V_LAM:V_LAM + NC], -1.0, None, ALU.mult))
            link(dve.tensor_tensor(soft, nlam, vec[:, V_LAM:V_LAM + NC], ALU.max))
            dve.wait_ge(lam_loaded, 64)
            link(dve.tensor_tensor(lam4[:, 0:4:2, :], lam4[:, 0:4:2, :], lam4[:, 1:4:2, :], ALU.mult))
            dve.tensor_reduce(small[:, LAM:LAM + 2], lam4[:, 0:4:2, :], AX_X, ALU.add).then_inc(setup1, 1)
            dve.wait_ge(setup2, 1)
            link(dve.tensor_tensor(small[:, LAM + 4:LAM + 5], small[:, LAM + 3:LAM + 4], small[:, LAM + 2:LAM + 3],
                                   ALU.subtract))
            link(dve.tensor_scalar(small[:, LAM + 5:LAM + 6], small[:, LAM + 4:LAM + 5], -LAM_INIT, None, ALU.add))
            u, s1, s2, ser = (small[:, SOFT + 4 * k:SOFT + 4 * k + 4] for k in (1, 3, 4, 5))
            link(dve.tensor_scalar(s2, u, 2.0, None, ALU.add))
            link(dve.reciprocal(s2, s2))
            link(dve.tensor_tensor(s1, u, s2, ALU.mult))
            link(dve.tensor_tensor(s2, s1, s1, ALU.mult))
            link(dve.tensor_scalar(ser, s2, 1.0 / 17, None, ALU.mult))
            for k in (15, 13, 11, 9, 7, 5, 3):
                link(dve.scalar_tensor_tensor(ser, ser, 1.0 / k, s2, ALU.add, ALU.mult))
            link(dve.scalar_tensor_tensor(ser, ser, 1.0, s1, ALU.add, ALU.mult))
            link(dve.tensor_scalar(nlam, nlam, 0.0, None, ALU.max))
            link(dve.scalar_tensor_tensor(ser, ser, 2.0, nlam, ALU.mult, ALU.add))
            link(dve.tensor_scalar(vec[:, V_HL:V_HL + NC], ser, LRU_C / 2, None, ALU.mult))
            link(dve.tensor_scalar(vec[:, V_NHL:V_NHL + NC], ser, -LRU_C / 2, None, ALU.mult))
            link(dve.tensor_scalar(vec[:, V_HB:V_HB + 2 * NC], vec[:, V_BA:V_BA + 2 * NC], 0.5, None, ALU.mult))
            link(dve.tensor_scalar(vec[:, V_Q8:V_Q8 + 1], vec[:, V_QG:V_QG + 1], float(HD) ** -0.5, None, ALU.mult))
            dve.tensor_scalar(vec[:, V_S8:V_S8 + 1], vec[:, V_SG:V_SG + 1], 1.0 - LAM_INIT, None, ALU.mult)\
                .then_inc(setup3, 1)
            dve.wait_ge(setup3, 1)

            def conv(c):
                wait_z(dve, c)
                y, z = h_rnn[:, c, :], acc[:, c % 4, :]

                def tap(j):
                    return vec[:, V_CW + NC * j + c:V_CW + NC * j + c + 1]
                link(dve.tensor_scalar(y, z, tap(CW - 1), vec[:, V_CB + c:V_CB + c + 1], ALU.mult, ALU.add))
                for back in range(1, CW):
                    ins = dve.scalar_tensor_tensor(y[:, back:T], z[:, 0:T - back], tap(CW - 1 - back), y[:, back:T],
                                                   ALU.mult, ALU.add)
                    if back < CW - 1:
                        link(ins)
                ins.then_inc(conv_done, 1)

            def lru(c):
                dve.wait_ge(gate_read, c + 1)
                dve.wait_ge(conv_done, c + 1)
                link(dve.scalar_tensor_tensor(iw[:], iw[:], 1.0, h_rnn[:, c, :], ALU.add, ALU.mult))
                dve.wait_ge(lns_ready, c + 1)
                dve.tensor_tensor(rt[:], rt[:], l1[:], ALU.subtract).then_inc(lnd_ready, 1)
                dve.wait_ge(mul_ready, c + 1)
                link(dve.tensor_tensor(iw[:], iw[:], l1[:], ALU.mult))
                dve.tensor_tensor_scan(h_rnn[:, c, :], decay[:], iw[:], 0.0, ALU.mult, ALU.add).then_inc(h_done, 1)

            def gelu(c):
                z = acc[:, (AT_G + c) % 4, :]
                dve.wait_ge(gsq_ready, c + 1)
                link(dve.tensor_scalar(ga[:], ga[:], 0.044715, 1.0, ALU.mult, ALU.add))
                dve.tensor_tensor(ga[:], z, ga[:], ALU.mult).then_inc(garg_ready, 1)
                dve.wait_ge(gth_ready, c + 1)
                link(dve.scalar_tensor_tensor(gb[:], gb[:], 1.0, z, ALU.add, ALU.mult))
                dve.wait_ge(h_done, c + 1)
                dve.scalar_tensor_tensor(gb[:], gb[:], 0.5, h_rnn[:, c, :], ALU.mult, ALU.mult).then_inc(yr_ready, 1)
                dve.wait_ge(yr_hi_ready, c + 1)
                dve.tensor_tensor(yr_lo[:, c, :], gb[:], yr_hi[:, c, :].bitcast(F32), ALU.subtract)\
                    .then_inc(yr_lo_ready, 1)

            def qk_norm(s):
                n, z = head_of(s), acc[:, s % 4, :]
                dve.wait_ge(qrs_ready, n + 1)
                if n < NH:
                    dve.scalar_tensor_tensor(k_sb[:, n, :], z, vec[:, V_KG:V_KG + 1], qrs[:], ALU.mult, ALU.mult)\
                        .then_inc(qk_done, 1)
                    return
                dve.wait_ge(qm_zero, 2)
                for c in range(2):
                    r = slice(HD * c, HD * c + HD)
                    ins = dve.scalar_tensor_tensor(qm[c][r, n - NH, :], z[r, :], vec[r, V_Q8:V_Q8 + 1], qrs[r, :],
                                                   ALU.mult, ALU.mult)
                ins.then_inc(qk_done, 1)

            for s, (kind, n) in enumerate(STEPS):
                if s in SPLIT:
                    lo_part(pre_chunk(SPLIT[s]))
                if kind == "x":
                    conv(n)
                if kind == "g":
                    gelu(n)
                if head_of(s - 1) is not None:
                    qk_norm(s - 1)
                if s in GATES:
                    lru(GATES[s])

            def scores_max(a):
                s, w = 2 * (a % 2), P * (a // NH + 1)
                dve.wait_ge(sc_ready, a + 1)
                dve.tensor_reduce(small[:, NMAX + s:NMAX + s + 2], acc[:, s:s + 2, 0:w], AX_X, ALU.max, negate=True)\
                    .then_inc(max_ready, 1)

            def weight_diff(a):
                s, w = 2 * (a % 2), P * (a // NH + 1)
                total, inv = small[:, SUMS + s:SUMS + s + 2], small[:, INV + s:INV + s + 2]
                dve.wait_ge(exp_done, 2 * a + 2)
                if a >= 2:
                    dve.wait_ge(wt_ps, a - 1)
                link(dve.reciprocal(inv, total))
                link(dve.scalar_tensor_tensor(inv[:, 1:2], inv[:, 1:2], small[:, LAM + 5:LAM + 6], total[:, 0:1],
                                              ALU.mult, ALU.mult))
                dve.scalar_tensor_tensor(wdiff[a % 2][:, 0:w], prob[a % 2][:, 1, 0:w], inv[:, 1:2],
                                         prob[a % 2][:, 0, 0:w], ALU.mult, ALU.add).then_inc(wd_ready, 1)

            for s in range(NA + 7):
                if s == 1:
                    lo_part(pre_chunk(PRE - 1))
                if s < NA:
                    scores_max(s)
                if 1 <= s <= NA:
                    weight_diff(s - 1)
                if s >= 9 and s % NH == 1:
                    b = (s - 9) // NH
                    dve.wait_ge(ors_ready, b + 1)
                    if b >= 1:
                        dve.wait_ge(ya_lo_ready, b)
                    dve.scalar_tensor_tensor(ya[:], o_c[:], vec[:, V_S8:V_S8 + 1], o_rs[:], ALU.mult, ALU.mult)\
                        .then_inc(ya_ready, 1)
                if s >= 10 and s % NH == 2:
                    b = (s - 10) // NH
                    dve.wait_ge(ya_hi_ready, b + 1)
                    dve.tensor_tensor(ya_lo[:, :, P * b:P * b + P], ya[:].rearrange("p (h n) -> p h n", h=NH),
                                      ya_hi[:, :, P * b:P * b + P].bitcast(F32), ALU.subtract).then_inc(ya_lo_ready, 1)

            def add_mix(t, g):
                wait_mix(dve, t, g)
                dst = xres[:, t, 512 * g:512 * g + 512]
                dve.tensor_tensor(dst, acc[:, 2 * (t % 2) + g, :], dst, ALU.add).then_inc(x1_done, 1)

            def choose(t):
                by_e, col = "p k e -> p e k", route[:, :, t, :]
                dve.wait_ge(lg_ps, t + 1)
                link(dve.max(top8[:], acc[:, 7, 0:E]))
                link(dve.max_index(idx8[:], top8[:], acc[:, 7, 0:E]))
                dve.tensor_scalar(g4[:, 6:7], top8[:, 0:1], -1.0, None, ALU.mult).then_inc(top_ready, 1)
                four = [P, TOP_K, E]
                link(dve.tensor_tensor(pick[:], iota_e[:].unsqueeze(1).broadcast_to(four),
                                       idx8[:, 0:TOP_K].unsqueeze(2).broadcast_to(four), ALU.is_equal))
                dve.tensor_reduce(chosen[:, t, :], pick[:].rearrange(by_e), AX_X, ALU.max).then_inc(tile_routed, 1)
                link(dve.scalar_tensor_tensor(which[:], pick[:, 2, :], 2.0, pick[:, 1, :], ALU.mult, ALU.add))
                dve.scalar_tensor_tensor(col[:, :, 6], pick[:, 3, :], 3.0, which[:], ALU.mult, ALU.add)
                dve.wait_ge(g4_ready, t + 1)
                link(dve.reciprocal(g4[:, 5:6], g4[:, 4:5]))
                link(dve.tensor_tensor(pickg[:], pick[:], g4[:, 0:TOP_K].unsqueeze(2).broadcast_to(four), ALU.mult))
                link(dve.tensor_reduce(rest[:], pickg[:].rearrange(by_e), AX_X, ALU.add))
                link(dve.tensor_scalar(gates[:, t, :], rest[:], g4[:, 5:6], None, ALU.mult))
                link(dve.tensor_copy(col[:, :, 8], gates[:, t, :]))
                link(dve.tensor_tensor(rest[:], gates[:, t, :], col[:, :, 8], ALU.subtract))
                link(dve.tensor_copy(col[:, :, 9], rest[:]))
                link(dve.tensor_tensor(col[:, :, 10], rest[:], col[:, :, 9], ALU.subtract))

            def h2t_half(t):
                dve.wait_ge(h2t_ps, 2 * t + 2)
                if t >= 2:
                    dve.wait_ge(lgt_ps, t - 1)
                dve.tensor_copy(h2_t[t % 2][:, 4:8, :], acc[:, 5, :].rearrange("p (k n) -> p k n", k=4))\
                    .then_inc(h2t_vec, 1)

            dve.wait_ge(gain_loaded, 32)
            dve.wait_ge(consts_ready, 1)
            dve.wait_ge(route_zero, 1)
            for t in range(NT):
                add_mix(t, 0)
                if t >= 1:
                    h2t_half(t - 1)
                if t >= 2:
                    choose(t - 2)
                add_mix(t, 1)
                dve.wait_ge(rstd2, t + 1)
                if t >= 2:
                    dve.wait_ge(h2_stored[t - 2], 16)
                dve.scalar_tensor_tensor(h2[t % 2][:], xres[:, t, :], small[:, RS + t:RS + t + 1], gain[:],
                                         ALU.mult, ALU.mult).then_inc(h2_ready, 1)
            h2t_half(NT - 1)
            for t in range(NT - 2, NT):
                choose(t)

            def mark(n, e):
                for t in range(NT):
                    dve.tensor_scalar(onehot[:, t, :], iota_slot[:], item_off[:, bass.ds(n, 1)],
                                      pos[:, bass.ds(e, 1), t], ALU.add, ALU.is_equal)
                dve.tensor_copy(rcur[:], route[:, bass.ds(e, 1), :, :].rearrange("p o t c -> p (o t) c"))\
                    .then_inc(onehot_ready, 1)

            def learn(n):
                dve.wait_ge(learned_ps, n + 1)
                dve.tensor_reduce(learned[:], acc[:, 7, 0:12].rearrange("p (a b) -> p a b", b=4), AX_X, ALU.add)\
                    .then_inc(learned_ready, 1)
                dve.wait_ge(learned_ready, n + 1)
                dve.wait_ge(gathered, n * 16)
                dve.tensor_scalar(tok_idx[:], learned[:, 0:1], BIG, None, ALU.add).then_inc(idx_ready, 1)

            dve.wait_ge(rank_ps, 1)
            link(dve.scalar_tensor_tensor(pos[:], acc[:, 6, 0:NT * E].rearrange("p (t e) -> p e t", e=E), 1.0,
                                          chosen[:].rearrange("p t e -> p e t"), ALU.add, ALU.mult))
            link(dve.tensor_scalar(pos[:], pos[:], -1.0, None, ALU.add))
            mark(0, 0)
            link(dve.tensor_copy(cnt[:, 0, :], acc[:, 6, NT * E:NT * E + E]))
            learn(0)
            for c in range(BEGUN):
                lo_part(item_chunk(0, c))
            more, total = cnt[:, 1, :], cnt[:, 2, :]
            link(dve.tensor_scalar(more, cnt[:, 0, :], float(SLOTS), None, ALU.is_gt))
            for m in range(2, T // SLOTS):
                link(dve.scalar_tensor_tensor(more, cnt[:, 0, :], float(SLOTS * m), more, ALU.is_gt, ALU.add))
            link(dve.memset(cnt[:, 3, :], 1.0))
            link(dve.tensor_tensor_scan(total, cnt[:, 3, :], more, 0.0, ALU.mult, ALU.add))
            wide = [P, EXTRA, E]
            link(dve.tensor_tensor(xtr[:, 0], total.unsqueeze(1).broadcast_to(wide), jot[:], ALU.is_le))
            link(dve.tensor_tensor(xtr[:, 1], xtr[:, 0], more.unsqueeze(1).broadcast_to(wide), ALU.mult))
            link(dve.tensor_reduce(xj[:, 0:2, :], xtr[:], AX_X, ALU.add))
            link(dve.tensor_scalar(item_e[:, E:ITEMS], xj[:, 0, :], float(E - 1), None, ALU.min))
            link(dve.tensor_copy(item_e[:, 0:E], iota_e[:]))
            link(dve.tensor_tensor(xj[:, 2, :], jot[:, :, 0], xj[:, 1, :], ALU.subtract))
            link(dve.tensor_scalar(xj[:, 2, :], xj[:, 2, :], 1.0, float(SLOTS), ALU.add, ALU.mult))
            link(dve.tensor_scalar(xj[:, 3, :], xj[:, 0, :], float(E), BIG, ALU.is_ge, ALU.mult))
            link(dve.tensor_tensor(item_off[:, E:ITEMS], xj[:, 2, :], xj[:, 3, :], ALU.add))
            dve.tensor_scalar(item_e[:, ITEMS:ITEMS + 1], total[:, E - 1:E], float(E), None, ALU.add)\
                .then_inc(tables_ready, 1)
            dve.wait_ge(tables_ready, 1)

            def shift(n):
                dve.tensor_copy(y_gate[:], held[:, 1:2]).then_inc(shift_own, 1)
                dve.tensor_scalar(y_idx[:], held[:, 0:1], BIG, None, ALU.add).then_inc(shift_own, 1)
                dve.wait_ge(shift_own, n * 2 + 2)
                dve.tensor_copy(held[:], learned[:, 1:3]).then_inc(shifted, 1)

            def xt_lo_half(g, hi_count):
                dve.wait_ge(xt_hi_ready, hi_count)
                dve.tensor_tensor(xt_lo[:, 4 * g:4 * g + 4, :], acc[:, 7, :].rearrange("p (k n) -> p k n", k=4),
                                  xt_hi[:, 4 * g:4 * g + 4, :].bitcast(F32), ALU.subtract).then_inc(xt_lo_ready, 1)

            dve.wait_ge(rows_zero, NT + 5)
            shift(0)
            for g in range(2):
                xt_lo_half(g, g + 1)
            def swiglu(i, half):
                dve.wait_ge(chunk_used, i * PER + PRE + 4 * half + 4)
                dve.tensor_scalar(gate_c[:], acc[:, 2 * half, :], LIMIT, None, ALU.min).then_inc(gate_ready, 1)
                dve.tensor_scalar(up_c[:], acc[:, 2 * half + 1, :], LIMIT, -LIMIT, ALU.min, ALU.max)\
                    .then_inc(up_ready, 1)
                dve.wait_ge(up_ready, i * 4 + 2 * half + 1)
                dve.wait_ge(gate_ready, i * 2 + half + 1)
                dve.scalar_tensor_tensor(up_c[:], up_c[:], 1.0, gate_c[:], ALU.add, ALU.mult).then_inc(up_ready, 1)
                dve.wait_ge(up_ready, i * 4 + 2 * half + 2)
                dve.wait_ge(sig_ready, i * 2 + half + 1)
                dve.tensor_tensor(act[half][:], up_c[:], sig[:], ALU.mult).then_inc(act_ready, 1)

            def at_lo_half(i, half):
                dve.wait_ge(at_hi_ready, i * 2 + half + 1)
                dve.tensor_tensor(at_lo[half][:], acc[:, 6, :].rearrange("p (k n) -> p k n", k=4),
                                  at_hi[half][:].bitcast(F32), ALU.subtract).then_inc(at_lo_ready, 1)

            def item(i, begun=0):
                for c in range(PER):
                    if c == 7:
                        swiglu(i, 0)
                    if c == 11:
                        swiglu(i, 1)
                        xt_lo_half(0, i * 2 + 3)
                        at_lo_half(i, 1)
                    if c >= begun:
                        lo_part(item_chunk(i, c))
                    if c == 1:
                        e = dve.value_load(item_e[0:1, bass.ds(i + 1, 1)], min_val=0, max_val=E - 1)
                        mark(i + 1, e)
                    if c == 3:
                        learn(i + 1)
                    if c == 8:
                        at_lo_half(i, 0)
                xt_lo_half(1, i * 2 + 4)
                dve.wait_ge(y_stored, i * 16 + 16)
                shift(i + 1)

            n_items = load_n_items(dve)
            item(0, BEGUN)
            with dve.Fori(1, n_items) as i:
                item(i)

            for t in range(NT):
                dve.wait_ge(gt_ps, NT)
                dve.tensor_copy(g_t[t][0:E, :], acc[0:E, 6, P * t:P * t + P]).then_inc(gt_ready, 1)
            for t in range(NT):
                for h in range(2):
                    dve.wait_ge(b2_ps, 2 * t + h + 1)
                    dst = xres[:, t, 512 * h:512 * h + 512]
                    dve.tensor_tensor(dst, acc[:, 2 * (t % 2) + h, :], dst, ALU.add).then_inc(b2_added, 1)
            for t in range(NT):
                dve.wait_ge(b2_added, 2 * NT)
                for k in range(TOP_K):
                    if k % 2 == 0:
                        dve.wait_ge(y4_loaded[2 * t + k // 2], 16)
                    ins = dve.tensor_tensor(xres[:, t, :], xres[:, t, :], columns(raw[2 * t + k // 2], 2)[:, k % 2, :], ALU.add)
                    if k < TOP_K - 1:
                        ins.then_inc(sum_own, 1)
                        dve.wait_ge(sum_own, 3 * t + k + 1)
                    else:
                        ins.then_inc(out_ready, 1)

        @block.tensor
        def _(pe):
            def wait_split(chunk):
                pe.wait_ge(lo_vec, chunk[0] + 1)
                pe.wait_ge(lo_pool, chunk[0] + 1)

            pe.wait_ge(ident_ready, 1)
            for t in range(NT):
                pe.wait_ge(xs_ready, t + 1)
                for g in range(2):
                    if 2 * t + g >= 7:
                        pe.wait_ge(ht_lo_ready, 2 * t + g - 6)
                    for k in range(4):
                        ins = pe.transpose(acc[:, (2 * t + g) % 7, P * k:P * k + P],
                                           xs[t % 2][:, P * (4 * g + k):P * (4 * g + k) + P], ident[:])
                    ins.then_inc(xt_ps, 1)
            pe.wait_ge(vecs_loaded, 16 * 9)
            pe.transpose(acc[:, 7, 0:64], vec_rows, ident[0:64, 0:64]).then_inc(vec_t, 1)

            def z_step(s):
                kind, n = STEPS[s]
                chunk = pre_chunk(CHUNK[s])
                if s == 0 or LAST[s - 1]:
                    wait_split(chunk)
                if s == 0:
                    pe.wait_ge(ht_lo_ready, 2 * NT)
                if s >= 4:
                    wait_z_read(pe, s - 4)
                for k in range(KD):
                    if kind == "v":
                        t = n % NT
                        stationary, dst = [m[:, k, P * t:P * t + P] for m in (ht_hi, ht_lo)], acc[:, s % 4, 0:CC]
                        moving = [m[:, k, :] for m in parts(chunk)]
                    else:
                        col = P * (n % 2)
                        stationary, dst = [m[:, k, col:col + P] for m in parts(chunk)], acc[:, s % 4, :]
                        moving = [m[:, k, :] for m in (ht_hi, ht_lo)]
                    ins = three_passes(pe, dst, stationary, moving, k == 0, k == KD - 1)
                ins.then_inc(chunk_used if LAST[s] else z_ready, 1)

            def lru_gate(c):
                pe.wait_ge(conv_done, c + 1)
                pe.wait_ge(bd_loaded, 64)
                if c >= 1:
                    pe.wait_ge(gate_read, c)
                pe.matmul(acc[:, 4, :], bd[:, c, :], h_rnn[:, c, :], start=True, stop=True)
                pe.matmul(acc[:, 5, :], bd[:, NC + c, :], h_rnn[:, c, :], start=True, stop=True).then_inc(gates_ready, 1)

            def head_squares(n):
                pe.wait_ge(qsq_ready, n + 1)
                pe.wait_ge(consts_ready, 1)
                if n >= 1:
                    pe.wait_ge(qrs_ready, n)
                pe.matmul(acc[:, 6, :], half_ones[:], (ga, gb, rt, l1)[n // NH * 2 + n % 2][:], start=True, stop=True)\
                    .then_inc(qss_ready, 1)

            def scores(a):
                b, h = a // NH, a % NH
                w = P * (b + 1)
                if a == 0:
                    pe.wait_ge(qk_done, 2 * NH)
                if a < 2:
                    pe.wait_ge(v_done, NT + 2 * a + 2)
                else:
                    pe.wait_ge(exp_done, 2 * (a - 1))
                for c in range(2):
                    dst = acc[:, 2 * (a % 2) + c, 0:w]
                    pe.matmul(dst, qm[c][:, h, P * b:P * b + P], k_sb[:, h, 0:w], start=True, stop=False)
                    ins = pe.matmul(dst[:, w - P:w], ident_bf[:], causal[:], start=False, stop=True)
                ins.then_inc(sc_ready, 1)

            for s in range(len(STEPS)):
                z_step(s)
                if s in GATES:
                    lru_gate(GATES[s])
                if head_of(s - 1) is not None:
                    head_squares(head_of(s - 1))

            def turn_weights(a):
                pe.wait_ge(ws_ready, a + 1)
                if a >= 2:
                    pe.wait_ge(wt_ready, a - 1)
                for k in range(a // NH + 1):
                    ins = pe.transpose(acc[:, 4 + a % 2, P * k:P * k + P], wdiff[a % 2][:, P * k:P * k + P], ident[:])
                ins.then_inc(wt_ps, 1)

            def times_v(a):
                b, h = a // NH, a % NH
                pe.wait_ge(wt_ready, a + 1)
                if b == 0:
                    pe.wait_ge(qrs_ready, 2 * NH)
                if h == 0 and b >= 2:
                    pe.wait_ge(ors_ready, b - 1)
                for k in range(b + 1):
                    ins = pe.matmul(acc[:, 6 + b % 2, P * h:P * h + P], v_sb[:, k, P * h:P * h + P],
                                    w_t[a % 2][:, P * k:P * k + P], start=(k == 0), stop=(k == b))
                ins.then_inc(o_ready, 1)

            def o_sums(b):
                pe.wait_ge(osq_ready, 2 * b + 2)
                pe.matmul(acc[:, 6 + b % 2, :], ones[:], o_sq[:], start=True, stop=True).then_inc(oss_ready, 1)

            for s in range(NA + 3):
                if s < NA:
                    scores(s)
                if 2 <= s <= NA + 1:
                    turn_weights(s - 2)
                if s >= 3:
                    times_v(s - 3)
                if s >= 7 and s % NH == 3:
                    o_sums((s - 7) // NH)

            def mix_half(t, g):
                if t == 0:
                    pe.wait_ge(exp_done, 2 * NA)
                if t >= 2:
                    pe.wait_ge(x1_done, 2 * (t - 2) + g + 1)
                pe.wait_ge(ya_lo_ready, t + 1)
                for j in range(2 * g, 2 * g + 2):
                    chunk = pre_chunk(N_IN + j)
                    wait_split(chunk)
                    for k in range(KD):
                        w = [m[:, k, :] for m in parts(chunk)]
                        pair, c = ((yr_hi, yr_lo), k) if k < NC else ((ya_hi, ya_lo), k - NC)
                        y = [m[:, c, P * t:P * t + P] for m in pair]
                        ins = three_passes(pe, acc[:, 2 * (t % 2) + g, CC * (j % 2):CC * (j % 2) + CC], y, w,
                                           k == 0, k == KD - 1)
                    if t == NT - 1:
                        ins.then_inc(chunk_used, 1)
                if t < NT - 1:
                    ins.then_inc(mix_ready, 1)

            def turn_h2(t):
                pe.wait_ge(h2_ready, t + 1)
                if t >= 1:
                    pe.wait_ge(h2t_act, t)
                    pe.wait_ge(h2t_vec, t)
                for g in range(2):
                    for k in range(4):
                        ins = pe.transpose(acc[:, 4 + g, P * k:P * k + P], h2[t % 2][:, P * (4 * g + k):P * (4 * g + k) + P],
                                           ident[:])
                    ins.then_inc(h2t_ps, 1)

            def logits(t):
                pe.wait_ge(rw_loaded, 16)
                pe.wait_ge(h2t_act, t + 1)
                pe.wait_ge(h2t_vec, t + 1)
                if t >= 1:
                    pe.wait_ge(lgt_ready, t)
                for k in range(KD):
                    ins = pe.matmul(acc[0:E, 6, 0:P], rw[:, k, :], h2_t[t % 2][:, k, :], start=(k == 0), stop=(k == KD - 1))
                ins.then_inc(lgt_ps, 1)

            def turn_logits(t):
                pe.wait_ge(lgt_ready, t + 1)
                if t >= 1:
                    pe.wait_ge(top_ready, t)
                pe.transpose(acc[:, 7, 0:E], lg_t[:], ident[0:E, 0:E]).then_inc(lg_ps, 1)

            pe.wait_ge(yr_lo_ready, NC)
            for t in range(NT):
                mix_half(t, 0)
                if t == 0:
                    o_sums(NT - 1)
                if t >= 1:
                    turn_h2(t - 1)
                if t >= 2:
                    turn_logits(t - 2)
                mix_half(t, 1)
                if t >= 1:
                    logits(t - 1)
            turn_logits(NT - 2)
            turn_h2(NT - 1)
            logits(NT - 1)
            turn_logits(NT - 1)

            pe.wait_ge(tile_routed, NT)
            for t in range(NT):
                for s in range(t):
                    pe.matmul(acc[:, 6, E * t:E * t + E], ones_bf[:], chosen[:, s, :], start=(s == 0), stop=False)
                pe.matmul(acc[:, 6, E * t:E * t + E], before[:], chosen[:, t, :], start=(t == 0), stop=True)
            for s in range(NT):
                ins = pe.matmul(acc[:, 6, E * NT:E * NT + E], ones_bf[:], chosen[:, s, :], start=(s == 0), stop=(s == NT - 1))
            ins.then_inc(rank_ps, 1)

            def learn(n):
                pe.wait_ge(onehot_ready, n + 1)
                for t in range(NT):
                    ins = pe.matmul(acc[:, 7, 0:12], onehot[:, t, :], rcur[:, t, :], start=(t == 0), stop=(t == NT - 1))
                ins.then_inc(learned_ps, 1)

            def turn_xg(g):
                for k in range(4):
                    ins = pe.transpose(acc[:, 7, P * k:P * k + P], xg[:, P * (4 * g + k):P * (4 * g + k) + P], ident[:])
                ins.then_inc(xg_ps, 1)

            def turn_act(i, half):
                pe.wait_ge(act_ready, i * 2 + half + 1)
                for k in range(4):
                    ins = pe.transpose(acc[:, 6, P * k:P * k + P], act[half][:, P * k:P * k + P], ident[:])
                ins.then_inc(at_ps, 1)

            learn(0)
            pe.wait_ge(gathered, 16)
            pe.wait_ge(idx_ready, 1)
            turn_xg(0)
            pe.wait_ge(xt_lo_ready, 1)
            turn_xg(1)
            n_items = load_n_items(pe)
            with pe.Fori(0, n_items) as i:
                for c in range(PER):
                    chunk = item_chunk(i, c)
                    wait_split(chunk)
                    if c == 0:
                        pe.wait_ge(xt_lo_ready, i * 2 + 2)
                        pe.wait_ge(b1row_loaded, i * 16 + 16)
                    if c < 8:
                        half, rows, up = c // 4, c % 4 // 2, c % 2
                        if c % 4 == 0:
                            for g in range(2):
                                col = g * D + half * 512
                                ins = pe.matmul(acc[:, 2 * half + g, :], ones_bf[:], b1row[:, col:col + 512],
                                                start=True, stop=False)
                            if half:
                                ins.then_inc(b1row_used, 1)
                        for k in range(4):
                            w = [m[:, k, :] for m in parts(chunk, 4)]
                            xk = [m[:, 4 * rows + k, :] for m in (xt_hi, xt_lo)]
                            ins = three_passes(pe, acc[:, 2 * half + up, :], xk, w, False, rows == 1 and k == 3)
                    else:
                        half = (c - 8) // 2
                        if c % 2 == 0:
                            pe.wait_ge(at_lo_ready, i * 2 + half + 1)
                        if c == 8:
                            pe.wait_ge(y_copied, i + 1)
                        for k in range(2):
                            if c == 9 and k == 1:
                                turn_act(i, 1)
                            kk = 2 * (c % 2) + k
                            for n in range(2):
                                w = [m[:, k, 512 * n:512 * n + 512] for m in parts(chunk, 2)]
                                a = [m[half][:, kk, :] for m in (at_hi, at_lo)]
                                ins = three_passes(pe, acc[:, 4 + n, :], a, w, c == 8 and k == 0, c == 11 and k == 1)
                    ins.then_inc(chunk_used, 1)
                    if c == 2:
                        learn(i + 1)
                    if c == 5:
                        turn_act(i, 0)
                    if c == 7:
                        pe.wait_ge(gathered, i * 16 + 32)
                        turn_xg(0)
                    if c == 9:
                        pe.wait_ge(xt_lo_ready, i * 2 + 3)
                        turn_xg(1)

            pe.wait_ge(at_lo_ready, n_items * 2)
            for t in range(NT):
                pe.transpose(acc[0:E, 6, P * t:P * t + P], gates[:, t, :], ident[:]).then_inc(gt_ps, 1)
            pe.wait_ge(b2_loaded, 16)
            pe.wait_ge(gt_ready, NT)
            for t in range(NT):
                for h in range(2):
                    if t >= 2:
                        pe.wait_ge(b2_added, 2 * (t - 2) + h + 1)
                    pe.matmul(acc[:, 2 * (t % 2) + h, :], g_t[t][:], b2_sb[:, 512 * h:512 * h + 512],
                              start=True, stop=True).then_inc(b2_ps, 1)


_INS = ["x", "norm1_g", "w_in", "conv_w", "conv_b", "lru_wa", "lru_ba", "lru_wx", "lru_bx", "lru_lambda",
        "q_norm_g", "k_norm_g", "lambda_q1", "lambda_k1", "lambda_q2", "lambda_k2", "subln_g", "w_out",
        "norm2_g", "router_w", "router_b", "w1", "b1", "w2", "b2"]


def kernel(**inputs):
    import numpy as np
    import concourse.bacc as bacc
    from concourse.bass_utils import run_bass_kernel_spmd

    nc = bacc.Bacc("TRN2", target_bir_lowering=False, num_devices=1)
    arrays, args = {}, []
    for name in _INS:
        a = np.ascontiguousarray(inputs[name])
        arrays[f"in_{name}"] = a
        args.append(nc.dram_tensor(f"in_{name}", a.shape, mybir.dt.from_np(a.dtype), kind="ExternalInput").ap())
    out = nc.dram_tensor("out", arrays["in_x"].shape, F32, kind="ExternalOutput").ap()
    layer_kernel(nc, *args, out)
    return run_bass_kernel_spmd(nc, [arrays], core_ids=[0]).results[0]["out"]
```
